# Optimizing a Trainium2 kernel written in Bass

```python
import math
import jax, jax.numpy as jnp
from jax import lax
import numpy as np

D_MODEL = 1024
BATCH = 1
SEQ = 256
DEPTH = 2

CHUNK = 64
N_META = 16
NORM_EPS = 1e-6

N_A_LAYERS = DEPTH // 2
N_B_LAYERS = DEPTH - N_A_LAYERS
N_DENSE = (DEPTH + 1) // 2
N_MOE = DEPTH // 2

D_RNN = D_MODEL
N_RNN_BLOCKS = 8
RNN_BLOCK = D_RNN // N_RNN_BLOCKS
CONV_WIDTH = 4
LRU_C = 8.0

N_HEADS = 16
QK_NOPE = 64
QK_ROPE = 32
V_HEAD = 64
Q_LORA = 384
KV_LORA = 256
ROPE_THETA = 10000.0
Q_BLOCK = 128
ATTN_SCALE = 1.0 / math.sqrt(QK_NOPE + QK_ROPE)
MASK_VALUE = -1e30

D_FF = 2816
N_EXPERTS = 8
TOP_K = 2
D_FF_EXPERT = 3584

kernel_name = 'hybrid_rglru_mla_moe_yoco_trunk'

def rmsnorm(x, g):
    xf = x.astype(jnp.float32)
    y = xf * lax.rsqrt(jnp.mean(xf * xf, axis=-1, keepdims=True) + NORM_EPS)
    return (y * g.astype(jnp.float32)).astype(x.dtype)

def chunk_ids(pos):
    return jnp.where(pos < N_META, 0, 1 + (pos - N_META) // CHUNK)

def rope(x, cos, sin):
    xf = x.astype(jnp.float32)
    half = xf.shape[-1] // 2
    x1, x2 = xf[..., :half], xf[..., half:]
    out = jnp.concatenate([x1 * cos - x2 * sin, x2 * cos + x1 * sin], axis=-1)
    return out.astype(x.dtype)

def causal_depthwise_conv(x, w, b):
    c = x.shape[-1]
    xp = jnp.pad(x, ((0, 0), (CONV_WIDTH - 1, 0), (0, 0)))
    y = lax.conv_general_dilated(xp, w[:, None, :].astype(x.dtype), window_strides=(1,), padding='VALID',
                                 dimension_numbers=('NWC', 'WIO', 'NWC'), feature_group_count=c)
    return y + b

def rg_lru(x, w_a, b_a, w_i, b_i, lam):
    bsz, t, c = x.shape
    xb = x.reshape(bsz, t, N_RNN_BLOCKS, RNN_BLOCK)
    gate_r = jax.nn.sigmoid(jnp.einsum('btnc,ncd->btnd', xb, w_a).reshape(bsz, t, c) + b_a)
    gate_i = jax.nn.sigmoid(jnp.einsum('btnc,ncd->btnd', xb, w_i).reshape(bsz, t, c) + b_i)
    log_a = -LRU_C * gate_r.astype(jnp.float32) * jax.nn.softplus(-lam.astype(jnp.float32))
    a = jnp.exp(log_a)
    mult = jnp.sqrt(-jnp.expm1(2.0 * log_a))
    u = mult * (gate_i * x).astype(jnp.float32)

    def combine(left, right):
        a1, b1 = left
        a2, b2 = right
        return a1 * a2, a2 * b1 + b2

    _, h = lax.associative_scan(combine, (a, u), axis=1)
    return h.astype(x.dtype)

def recurrent_mixer(h, w_in, conv_w, conv_b, w_a, b_a, w_i, b_i, lam, w_out):
    proj = h @ w_in
    y_gate = jax.nn.gelu(proj[..., :D_RNN], approximate=True)
    x_rnn = causal_depthwise_conv(proj[..., D_RNN:], conv_w, conv_b)
    x_rnn = rg_lru(x_rnn, w_a, b_a, w_i, b_i, lam)
    return (x_rnn * y_gate) @ w_out

def shared_latent_kv(x, g_src, w_down, g_latent, w_up, cos, sin):
    bsz, t, _ = x.shape
    hs = rmsnorm(x, g_src)
    ckv = hs @ w_down
    c_lat = rmsnorm(ckv[..., :KV_LORA], g_latent)
    k_pe = rope(ckv[..., KV_LORA:], cos, sin)
    kv = (c_lat @ w_up).reshape(bsz, t, N_HEADS, QK_NOPE + V_HEAD)
    return kv[..., :QK_NOPE], k_pe, kv[..., QK_NOPE:]

def mla_mixer(h, k_nope, k_pe, v, w_dq, g_q, w_uq, w_o, cos, sin, cid):
    bsz, t, _ = h.shape
    c_q = rmsnorm(h @ w_dq, g_q)
    q = (c_q @ w_uq).reshape(bsz, t, N_HEADS, QK_NOPE + QK_ROPE)
    q_nope = q[..., :QK_NOPE]
    q_pe = rope(q[..., QK_NOPE:], cos[:, None, :], sin[:, None, :])
    n_blk = -(-t // Q_BLOCK)
    tp = n_blk * Q_BLOCK
    pad = ((0, 0), (0, tp - t), (0, 0), (0, 0))
    qn_b = jnp.pad(q_nope, pad).reshape(bsz, n_blk, Q_BLOCK, N_HEADS, QK_NOPE).transpose(1, 0, 2, 3, 4)
    qp_b = jnp.pad(q_pe, pad).reshape(bsz, n_blk, Q_BLOCK, N_HEADS, QK_ROPE).transpose(1, 0, 2, 3, 4)
    cid_q = chunk_ids(jnp.arange(tp)).reshape(n_blk, Q_BLOCK)

    def attend(args):
        qn, qp, cq = args
        s = (jnp.einsum('bqhd,bkhd->bhqk', qn, k_nope, preferred_element_type=jnp.float32)
             + jnp.einsum('bqhr,bkr->bhqk', qp, k_pe, preferred_element_type=jnp.float32)) * ATTN_SCALE
        mask = cid[None, :] <= cq[:, None]
        p = jax.nn.softmax(jnp.where(mask, s, MASK_VALUE), axis=-1).astype(v.dtype)
        return jnp.einsum('bhqk,bkhd->bqhd', p, v)

    o = lax.map(attend, (qn_b, qp_b, cid_q))
    o = o.transpose(1, 0, 2, 3, 4).reshape(bsz, tp, N_HEADS * V_HEAD)[:, :t]
    return o @ w_o

def swiglu(h, w1, w3, w2):
    return (jax.nn.silu(h @ w1) * (h @ w3)) @ w2

def moe_swiglu(h, w_router, w1, w3, w2):
    logits = (h @ w_router).astype(jnp.float32)
    top_v, top_i = lax.top_k(logits, TOP_K)
    gates = jax.nn.softmax(top_v, axis=-1)
    dense_gate = jnp.sum(jax.nn.one_hot(top_i, N_EXPERTS, dtype=jnp.float32) * gates[..., None], axis=-2)
    out = jnp.zeros(h.shape, jnp.float32)
    for e in range(N_EXPERTS):
        y = swiglu(h, w1[e], w3[e], w2[e]).astype(jnp.float32)
        out = out + dense_gate[..., e:e + 1] * y
    return out.astype(h.dtype)

def setup_inputs(seed: int = 0) -> dict:
    key = jax.random.key(seed)
    ks = jax.random.split(key, 32)
    f32 = jnp.float32

    def nrm(k, shape, fan_in):
        return jax.random.normal(k, shape, f32) * (fan_in ** -0.5)

    def gain(k, shape):
        return 1.0 + 0.02 * jax.random.normal(k, shape, f32)

    def small(k, shape):
        return 0.01 * jax.random.normal(k, shape, f32)

    u = jax.random.uniform(ks[12], (N_A_LAYERS, D_RNN), f32, minval=0.9, maxval=0.999)
    s = u ** (1.0 / LRU_C)
    return {
        'x': jax.random.normal(ks[0], (BATCH, SEQ, D_MODEL), f32),
        'meta_tokens': jax.random.normal(ks[1], (N_META, D_MODEL), f32),
        'norm_mix': gain(ks[2], (DEPTH, D_MODEL)),
        'norm_ffn': gain(ks[3], (DEPTH, D_MODEL)),
        'norm_final': gain(ks[4], (D_MODEL,)),
        'rnn_w_in': nrm(ks[5], (N_A_LAYERS, D_MODEL, 2 * D_RNN), D_MODEL),
        'rnn_conv_w': nrm(ks[6], (N_A_LAYERS, CONV_WIDTH, D_RNN), CONV_WIDTH),
        'rnn_conv_b': small(ks[7], (N_A_LAYERS, D_RNN)),
        'rnn_w_a': nrm(ks[8], (N_A_LAYERS, N_RNN_BLOCKS, RNN_BLOCK, RNN_BLOCK), RNN_BLOCK),
        'rnn_b_a': small(ks[9], (N_A_LAYERS, D_RNN)),
        'rnn_w_i': nrm(ks[10], (N_A_LAYERS, N_RNN_BLOCKS, RNN_BLOCK, RNN_BLOCK), RNN_BLOCK),
        'rnn_b_i': small(ks[11], (N_A_LAYERS, D_RNN)),
        'rnn_lambda': jnp.log(s) - jnp.log1p(-s),
        'rnn_w_out': nrm(ks[13], (N_A_LAYERS, D_RNN, D_MODEL), D_RNN),
        'kv_norm_src': gain(ks[14], (D_MODEL,)),
        'kv_w_down': nrm(ks[15], (D_MODEL, KV_LORA + QK_ROPE), D_MODEL),
        'kv_latent_norm': gain(ks[16], (KV_LORA,)),
        'kv_w_up': nrm(ks[17], (KV_LORA, N_HEADS * (QK_NOPE + V_HEAD)), KV_LORA),
        'q_w_down': nrm(ks[18], (N_B_LAYERS, D_MODEL, Q_LORA), D_MODEL),
        'q_latent_norm': gain(ks[19], (N_B_LAYERS, Q_LORA)),
        'q_w_up': nrm(ks[20], (N_B_LAYERS, Q_LORA, N_HEADS * (QK_NOPE + QK_ROPE)), Q_LORA),
        'attn_w_out': nrm(ks[21], (N_B_LAYERS, N_HEADS * V_HEAD, D_MODEL), N_HEADS * V_HEAD),
        'ffn_w1': nrm(ks[22], (N_DENSE, D_MODEL, D_FF), D_MODEL),
        'ffn_w3': nrm(ks[23], (N_DENSE, D_MODEL, D_FF), D_MODEL),
        'ffn_w2': nrm(ks[24], (N_DENSE, D_FF, D_MODEL), D_FF),
        'moe_router': nrm(ks[25], (N_MOE, D_MODEL, N_EXPERTS), D_MODEL),
        'moe_w1': nrm(ks[26], (N_MOE, N_EXPERTS, D_MODEL, D_FF_EXPERT), D_MODEL),
        'moe_w3': nrm(ks[27], (N_MOE, N_EXPERTS, D_MODEL, D_FF_EXPERT), D_MODEL),
        'moe_w2': nrm(ks[28], (N_MOE, N_EXPERTS, D_FF_EXPERT, D_MODEL), D_FF_EXPERT),
    }

def reference(x, meta_tokens, norm_mix, norm_ffn, norm_final, rnn_w_in, rnn_conv_w, rnn_conv_b,
              rnn_w_a, rnn_b_a, rnn_w_i, rnn_b_i, rnn_lambda, rnn_w_out, kv_norm_src, kv_w_down,
              kv_latent_norm, kv_w_up, q_w_down, q_latent_norm, q_w_up, attn_w_out,
              ffn_w1, ffn_w3, ffn_w2, moe_router, moe_w1, moe_w3, moe_w2):
    bsz = x.shape[0]
    meta = jnp.broadcast_to(meta_tokens.astype(x.dtype)[None], (bsz, N_META, x.shape[-1]))
    h = jnp.concatenate([meta, x], axis=1)
    t = h.shape[1]
    pos = jnp.arange(t)
    cid = chunk_ids(pos)
    inv_freq = ROPE_THETA ** (-jnp.arange(0, QK_ROPE, 2, dtype=jnp.float32) / QK_ROPE)
    ang = pos.astype(jnp.float32)[:, None] * inv_freq[None, :]
    cos, sin = jnp.cos(ang), jnp.sin(ang)

    k_nope = k_pe = v = None
    for layer in range(DEPTH):
        hn = rmsnorm(h, norm_mix[layer])
        if layer < N_A_LAYERS:
            a = layer
            h = h + recurrent_mixer(hn, rnn_w_in[a], rnn_conv_w[a], rnn_conv_b[a], rnn_w_a[a], rnn_b_a[a],
                                    rnn_w_i[a], rnn_b_i[a], rnn_lambda[a], rnn_w_out[a])
        else:
            b = layer - N_A_LAYERS
            if b == 0:
                k_nope, k_pe, v = shared_latent_kv(h, kv_norm_src, kv_w_down, kv_latent_norm, kv_w_up, cos, sin)
                hn = rmsnorm(h, norm_mix[layer])
            h = h + mla_mixer(hn, k_nope, k_pe, v, q_w_down[b], q_latent_norm[b], q_w_up[b],
                              attn_w_out[b], cos, sin, cid)
        hf = rmsnorm(h, norm_ffn[layer])
        if layer % 2 == 0:
            e = layer // 2
            h = h + swiglu(hf, ffn_w1[e], ffn_w3[e], ffn_w2[e])
        else:
            m = layer // 2
            h = h + moe_swiglu(hf, moe_router[m], moe_w1[m], moe_w3[m], moe_w2[m])
    h = rmsnorm(h, norm_final)
    return h[:, N_META:]


_drawn_inputs = setup_inputs


def setup_inputs(seed=0):
    import zlib

    import numpy as np

    out = dict(_drawn_inputs(seed))
    spreads = {}
    factors = {'norm_final': 2.876,
     'rnn_b_a': 5.016,
     'rnn_b_i': 8.0,
     'kv_norm_src': 4.387,
     'kv_latent_norm': 3.108,
     'q_latent_norm': 4.491}
    for name, (base, spread) in spreads.items():
        noise = np.random.default_rng([zlib.crc32(name.encode()), seed]).standard_normal(out[name].shape)
        drawn = base * np.exp(spread * noise) if base else spread * noise
        out[name] = __import__('jax').numpy.asarray(drawn.astype(out[name].dtype))
    for name, factor in factors.items():
        out[name] = (out[name] * factor).astype(out[name].dtype)
    return out
```

```python
from contextlib import ExitStack

import numpy as np

import concourse.bass as bass
from concourse import mybir

F32 = mybir.dt.float32
F32R = mybir.dt.float32r
BF16 = mybir.dt.bfloat16
I32 = mybir.dt.int32
ACT = mybir.ActivationFunctionType
ALU = mybir.AluOpType
AX = mybir.AxisListType

P = 128
D = 1024
KD = D // P
N_META = 16
SEQ = 256
T = N_META + SEQ
CHUNK = 64
TOKEN_TILES = [(0, 128), (128, 128), (256, 16)]
NT = len(TOKEN_TILES)
EPS = 1e-6
CONV = 4
N_BLOCKS = 8
LRU_C = 8.0
HEADS = 16
NOPE, ROPE, VH = 64, 32, 64
QH = NOPE + ROPE
Q_LORA, KV_LORA = 384, 256
KQ, KC = Q_LORA // P, KV_LORA // P
SCALE = float(1.0 / np.sqrt(QH))
MASK = -1e30
D_FF = 2816
KF = D_FF // P
N_EXPERTS = 8
TOP_K = 2
D_FFE = 3584

KEYS_OF_FIRST = 144
QUERIES_OF_SECOND = 64
QUERIES_OF_THIRD = 192

C_IDENT, C_TRI, C_IOTA, C_TIE = 0, 128, 256, 384
C_ROPE = 448
C_QMASK = C_ROPE + T
C_KMASK = C_QMASK + T
N_CONST = C_KMASK + T
N_CHUNKS = 1 + SEQ // CHUNK

PARAMS = [("norm_mix", 16), ("norm_ffn", 16), ("kv_src", 8), ("conv_w", 32), ("conv_b", 8),
          ("b_a", 8), ("b_i", 8), ("lam", 8), ("q_lat", 3), ("kv_lat", 2)]
PCOL = {}
_at = 0
for _name, _n in PARAMS:
    PCOL[_name] = _at
    _at += _n
N_PARAMS = _at

STEP = 512
STEPS = D_FFE // STEP
UNIT = 2048
RAW = 7
SPLIT = 3
UNITS = 6 * STEPS
PASSES = -(-T // P)
RUNS = N_EXPERTS * PASSES


def shape_constants():
    c = np.zeros((P, N_CONST), np.float32)
    i = np.arange(P)
    c[:, C_IDENT:C_IDENT + P] = np.eye(P)
    c[:, C_TRI:C_TRI + P] = i[:, None] < i[None, :]
    c[:, C_IOTA:C_IOTA + P] = i[None, :]
    e = np.arange(N_EXPERTS)
    c[:, C_TIE:C_TIE + 64] = (e[None, :] < e[:, None]).reshape(1, 64)
    half = ROPE // 2
    inv = (np.float32(10000.0) ** (-np.arange(0, ROPE, 2, dtype=np.float32) / np.float32(ROPE))).astype(np.float32)
    ang = (inv[:, None] * np.arange(T, dtype=np.float32)[None, :]).astype(np.float32)
    for o in (0, half):
        c[64 + o:64 + o + half, C_ROPE:C_ROPE + T] = np.cos(ang)
    c[96:96 + half, C_ROPE:C_ROPE + T] = -np.sin(ang)
    c[96 + half:96 + ROPE, C_ROPE:C_ROPE + T] = np.sin(ang)
    pos = np.arange(T)
    cid = np.where(pos < N_META, 0, 1 + (pos - N_META) // CHUNK)
    for n in range(N_CHUNKS):
        c[QH + n, C_QMASK:C_QMASK + T] = cid < n
        c[QH + n, C_KMASK:C_KMASK + T] = np.where(cid == n, MASK, 0.0)
    return c


class Units:

    def __init__(self):
        self.landed = [0, 0]
        self.arrived = []

    def add(self, n, dmas=1):
        first = len(self.arrived)
        for u in range(first, first + n):
            self.landed[u % 2] += 16 * dmas
            self.arrived.append(self.landed[u % 2])
        return first


def trunk(nc, x, meta_tokens, norm_mix, norm_ffn, norm_final, rnn_w_in, rnn_conv_w, rnn_conv_b,
          rnn_w_a, rnn_b_a, rnn_w_i, rnn_b_i, rnn_lambda, rnn_w_out, kv_norm_src, kv_w_down,
          kv_latent_norm, kv_w_up, q_w_down, q_latent_norm, q_w_up, attn_w_out, ffn_w1, ffn_w3,
          ffn_w2, moe_router, moe_w1, moe_w3, moe_w2, consts, out):
    ctx = ExitStack()
    with ctx:
        class Region:

            def __init__(self, at):
                self.at = at

            def sb(self, name, shape, dt=F32):
                n = (2 if dt == BF16 else 4) * int(np.prod(shape[1:]))
                t = nc.alloc_sbuf_tensor_at(name, shape, dt, offset=self.at)
                self.at += -(-n // 32) * 32
                return t

        base = -(-nc.sbuf_base // 64) * 64
        end = nc.sbuf_usable_end
        ctx.enter_context(nc.sbuf_tensor("slab", [P, (end - base) // 4 - 16], F32))

        fixed = Region(base)
        const = fixed.sb("const", [P, N_CONST])
        params = fixed.sb("params", [P, N_PARAMS])
        ones = fixed.sb("ones", [P, P])
        small = fixed.sb("small", [P, 2])
        eps = small[:, 0:1]
        count_i = fixed.sb("count_i", [P, 8], I32)
        router = fixed.sb("router", [P, KD, N_EXPERTS])
        sp_t = fixed.sb("sp_t", [P, 8, N_BLOCKS])
        split_at = fixed.at
        w_hi = fixed.sb("w_hi", [P, 2, 3072], F32R)
        w_lo = fixed.sb("w_lo", [P, 2, 3072], F32R)
        mixture_split = Region(split_at)
        m_hi = mixture_split.sb("m_hi", [P, SPLIT, UNIT], F32R)
        m_lo = mixture_split.sb("m_lo", [P, SPLIT, UNIT], F32R)
        raw_at = fixed.at
        m_raw = fixed.sb("m_raw", [P, RAW, UNIT])
        work_at = fixed.at

        rnn = Region(raw_at)
        x_pad = rnn.sb("x_pad", [P, KD, T + CONV - 1])
        x_conv = rnn.sb("x_conv", [P, KD, T])
        gate_r = rnn.sb("gate_r", [P, KD, T])
        gate_i = rnn.sb("gate_i", [P, KD, T])
        decay = rnn.sb("decay", [P, KD, T])
        tanh_z = rnn.sb("tanh_z", [P, KD, T])
        assert rnn.at <= work_at
        start = Region(raw_at + 2 * 8832)
        x_rows = start.sb("x_rows", [P, NT, D])
        p_rows = start.sb("p_rows", [P, P])
        ffn = Region(raw_at)
        g_hi = ffn.sb("g_hi", [P, KF, T], F32R)
        g_lo = ffn.sb("g_lo", [P, KF, T], F32R)
        silu = ffn.sb("silu", [P, 2, T])
        g_f32 = ffn.sb("g_f32", [P, 2, T])
        assert ffn.at <= work_at
        slot6 = Region(raw_at + (RAW - 1) * 4 * UNIT)
        latent_kv = slot6.sb("latent_kv", [P, KC, T])
        latent_q = slot6.sb("latent_q", [P, KQ, T])
        rope_a = slot6.sb("rope_a", [P, T])
        rope_b = slot6.sb("rope_b", [P, T])
        assert slot6.at <= work_at

        dense = Region(work_at)
        h = dense.sb("h", [P, KD, T])
        normed = dense.sb("normed", [P, KD, T])
        transition = dense.at
        raw = dense.sb("raw", [P, 2, 3072])
        std = dense.sb("std", [P, T])
        rstd = dense.sb("rstd", [P, T])
        sq = dense.sb("sq", [P, 4, T])
        a_at = dense.at
        a_hi = dense.sb("a_hi", [P, KD, T], F32R)
        a_lo = dense.sb("a_lo", [P, KD, T], F32R)
        b_at = dense.at
        b_hi = dense.sb("b_hi", [P, KD, T], F32R)
        b_lo = dense.sb("b_lo", [P, KD, T], F32R)
        y_gate = dense.sb("y_gate", [P, KD, T])
        assert dense.at <= end, (dense.at, end)
        att = Region(b_at + 2 * 4 * KD * T)
        c_hi = att.sb("c_hi", [P, KC, T], F32R)
        c_lo = att.sb("c_lo", [P, KC, T], F32R)
        cq_hi = att.sb("cq_hi", [P, KQ, T], F32R)
        cq_lo = att.sb("cq_lo", [P, KQ, T], F32R)
        k_head = att.sb("k_head", [P, 2, T])
        q_head = att.sb("q_head", [P, 2, T])
        n_max = att.sb("n_max", [P, 2, 4])
        bias_e = att.sb("bias_e", [P, 2, 4])
        p_sum = att.sb("p_sum", [P, 2, 4])
        p_inv = att.sb("p_inv", [P, 2, 4])
        assert att.at <= end, (att.at, end)
        probs_r = Region(b_at)
        v_sb = probs_r.sb("v_sb", [P, 2, NT, 4 * VH])
        prob0 = probs_r.sb("prob0", [P, 2, 256])
        prob1 = probs_r.sb("prob1", [P, 2, T])
        prob2 = probs_r.sb("prob2", [P, 2, T])
        probT = probs_r.sb("probT", [P, 2, T + 208])
        probT2 = probs_r.sb("probT2", [P, 2, 80])
        assert probs_r.at <= b_at + 2 * 4 * KD * T

        tokens_r = Region(transition)
        hf = tokens_r.sb("hf", [P, 3, NT, D], BF16)
        assert tokens_r.at <= a_at
        y_out = Region(transition).sb("y_out", [P, NT, D])
        moe = Region(a_at)
        acc = moe.sb("acc", [P, NT, D])
        g_final = moe.sb("g_final", [P, D])
        xe_hi = moe.sb("xe_hi", [P, KD, P], F32R)
        xe_lo = moe.sb("xe_lo", [P, KD, P], F32R)
        rest = Region(moe.at).sb("rest", [P, 2, STEP])
        silu_e = moe.sb("silu_e", [P, STEP])
        gated = moe.sb("gated", [P, STEP])
        gt_hi = moe.sb("gt_hi", [P, 2, 4, P], F32R)
        gt_lo = moe.sb("gt_lo", [P, 2, 4, P], F32R)
        routing = Region(moe.at)
        gate_rest = routing.sb("gate_rest", [P, NT, N_EXPERTS])
        logit = routing.sb("logit", [P, NT, N_EXPERTS])
        cmp_a = routing.sb("cmp_a", [P, NT, 64])
        cmp_b = routing.sb("cmp_b", [P, NT, 64])
        chosen = routing.sb("chosen", [P, NT, N_EXPERTS])
        gate = routing.sb("gate", [P, NT, N_EXPERTS])
        r_small = routing.sb("r_small", [P, 4, NT])
        r_exp = routing.sb("r_exp", [P, NT, N_EXPERTS])
        place_1 = routing.sb("place_1", [P, NT, N_EXPERTS])
        y_hi = moe.sb("y_hi", [P, D], F32R)
        y_lo = moe.sb("y_lo", [P, D], F32R)
        y_f32 = moe.sb("y_f32", [P, D])
        pick = moe.sb("pick", [P, NT, P], BF16)
        assert moe.at <= end, (moe.at, end)
        after = Region(base + 4 * C_ROPE)
        pickT = after.sb("pickT", [P, T], F32R)
        ident_b = after.sb("ident_b", [P, P], BF16)
        place = after.sb("place", [P, NT, RUNS + 2])
        gate_part = after.sb("gate_part", [P, 3, NT, N_EXPERTS], BF16)
        g_slot = after.sb("g_slot", [P, 1])
        ss = after.sb("ss", [P, 3, NT])
        assert after.at <= base + 4 * N_CONST

        banks = [ctx.enter_context(nc.psum_tensor(f"bank{i}", [P, 512], F32)) for i in range(8)]
        B = [b[:, :] for b in banks]

        names = {}

        def S(name):
            if name not in names:
                names[name] = ctx.enter_context(nc.semaphore(name))
            return names[name]

        def prm(name, k):
            c = PCOL[name] + k
            return params[:, c:c + 1]

        ident = const[:, C_IDENT:C_IDENT + P]

        units = Units()
        U_X = units.add(4)
        U_Y = units.add(4)
        U_G = units.add(1, 2)
        U_O = units.add(4)
        U_F = units.add(2 * (KF // 2))
        U_W2 = units.add(8)
        U_KV = units.add(1)
        U_Q = units.add(1)
        U_H = units.add(4, 2)
        U_AO = units.add(4)
        n_units = len(units.arrived)

        def src_cols(w, c, n):
            return w.rearrange("(k p) n -> p k n", p=P)[:, :, bass.ds(c, n)]

        w_in_v = rnn_w_in.rearrange("o a b -> (o a) b")
        w_out_v = rnn_w_out.rearrange("o a b -> (o a) b")
        f1_v = ffn_w1.rearrange("o a b -> (o a) b")
        f3_v = ffn_w3.rearrange("o a b -> (o a) b")
        f2_v = ffn_w2.rearrange("o a b -> (o a) b")
        qd_v = q_w_down.rearrange("o a b -> (o a) b")
        qu_v = q_w_up.rearrange("o a b -> (o a) b")
        ao_v = attn_w_out.rearrange("o a b -> (o a) b")

        def raw_v(s, n, k):
            return raw[:, s, 0:n].rearrange("p (k n) -> p k n", k=k)

        def dma_unit(sp_, u, slot, pieces):
            if not isinstance(u, int) or u >= 2:
                sp_.wait_ge(S("w_lo_ready"), u - 1)
            for dst, src in pieces:
                sp_.dma_start(dst, src).then_inc(S(f"w_landed{slot}"), 16)

        def load_256(sp_, u, slot, w, c):
            dma_unit(sp_, u, slot, [(raw_v(slot, 2048, 8), src_cols(w, c, 256))])

        def parts(kind, slot):
            r, hi, lo = raw[:, slot, :], w_hi[:, slot, :], w_lo[:, slot, :]
            if isinstance(kind, int):
                cut = -(-(kind // 2) // 256) * 256
                return [[(r[:, a:b], hi[:, a:b], lo[:, a:b])] for a, b in ((0, cut), (cut, kind))]
            if kind == "kv_down":
                rv = r[:, 0:8 * 288].rearrange("p (k n) -> p k n", k=8)
                dst = [w[:, 0:8 * 320].rearrange("p (k n) -> p k n", k=8) for w in (hi, lo)]
                moves = [(0, 288, 0), (272, 288, 288), (256, 272, 304)]
                views = [(rv[:, :, a:b], *(d[:, :, c:c + b - a] for d in dst)) for a, b, c in moves]
                return [views[:1], views[1:]]
            rv = r[:, 1024:1024 + 12 * QH].rearrange("p (k n) -> p k n", k=12)
            dst = [w[:, 1024:1024 + 12 * P].rearrange("p (k n) -> p k n", k=12) for w in (hi, lo)]
            moves = [(0, QH, 0), (NOPE + 16, QH, QH), (NOPE, NOPE + 16, QH + 16)]
            views = [(rv[:, :, a:b], *(d[:, :, c:c + b - a] for d in dst)) for a, b, c in moves]
            return [[(r[:, 0:1024], hi[:, 0:1024], lo[:, 0:1024])], views]

        def split_hi(act, u, slot, kind, arrived):
            act.wait_ge(S(f"w_landed{slot}"), arrived)
            if not isinstance(u, int) or u >= 2:
                act.wait_ge(S("w_used"), u - 1)
            for portion in parts(kind, slot):
                for r, hi, _ in portion:
                    last = act.activation(hi, r, ACT.Copy)
                last.then_inc(S("w_hi_ready"), 1)

        def split_lo(dve, u, slot, kind):
            for n, portion in enumerate(parts(kind, slot)):
                dve.wait_ge(S("w_hi_ready"), 2 * u + n + 1)
                for r, hi, lo in portion:
                    last = dve.tensor_tensor(lo, r, hi.bitcast(F32), ALU.subtract)
            last.then_inc(S("w_lo_ready"), 1)

        KIND = {}
        for first, n, kind in ((U_X, 9, 2048), (U_O, 4, 2048), (U_F, KF, 2048), (U_W2, 8, 11 * 256),
                               (U_KV, 1, "kv_down"), (U_Q, 1, 3072), (U_H, 4, "heads"), (U_AO, 4, 2048)):
            for u in range(first, first + n):
                KIND[u] = kind

        def hi_of(act, u):
            if u < n_units:
                split_hi(act, u, u % 2, KIND[u], units.arrived[u])

        def lo_of(dve, u):
            if u < n_units:
                split_lo(dve, u, u % 2, KIND[u])

        def three(pe, o, wh, wl, xh, xl, first, last):
            pe.matmul(o, wh, xh, start=first, stop=False)
            pe.matmul(o, wh, xl, start=False, stop=False)
            return pe.matmul(o, wl, xh, start=False, stop=last)

        def blocks_of(slot, n, k):
            return [w[:, slot, 0:n].rearrange("p (k n) -> p k n", k=k) for w in (w_hi, w_lo)]

        def two_products(pe, slot, banks2, xh, xl, block_ready):
            wh, wl = blocks_of(slot, 2048, KD)
            for k in range(KD):
                block_ready(k)
                for j, bank in enumerate(banks2):
                    cols = slice(P * j, P * (j + 1))
                    ins = three(pe, bank[:, 0:T], wh[:, k, cols], wl[:, k, cols], xh[:, k, :], xl[:, k, :],
                                k == 0, k == KD - 1)
            return ins

        def product(pe, slot, n, k, col, bank, xh, xl, x0=0, first=True, last=True, m=P):
            wh, wl = blocks_of(slot, n, k)
            for kk in range(k):
                ins = three(pe, bank[0:m, 0:T], wh[:, kk, col:col + m], wl[:, kk, col:col + m],
                            xh[:, x0 + kk, :], xl[:, x0 + kk, :], first and kk == 0, last and kk == k - 1)
            return ins

        def norm_square(act, tag, k, src):
            if k >= 4:
                act.wait_ge(S(f"{tag}_summed"), k - 3)
            act.activation(sq[:, k % 4, :], src, ACT.Square).then_inc(S(f"{tag}_squared"), 1)

        def norm_sum(pe, tag, k, n, bank):
            pe.wait_ge(S(f"{tag}_squared"), k + 1)
            pe.matmul(bank[:, 0:T], ones[:, :], sq[:, k % 4, :], start=k == 0,
                      stop=k == n - 1).then_inc(S(f"{tag}_summed"), 1)

        def norm_std(act, tag, n, bank):
            act.wait_ge(S(f"{tag}_summed"), n)
            act.activation(std[:, :], bank[:, 0:T], ACT.Sqrt, bias=eps,
                           scale=1.0 / (n * P)).then_inc(S(f"{tag}_std"), 1)

        def norm_inv(dve, tag):
            dve.wait_ge(S(f"{tag}_std"), 1)
            dve.reciprocal(rstd[:, :], std[:, :]).then_inc(S(f"{tag}_inv"), 1)
            dve.wait_ge(S(f"{tag}_inv"), 1)

        def norm_scale(dve, tag, n, src, gain, hi, lo):
            for k in range(n + 1):
                if k < n:
                    dve.scalar_tensor_tensor(normed[:, k, :], src[:, k, :], gain(k), rstd[:, :], ALU.mult,
                                             ALU.mult).then_inc(S(f"{tag}_scaled"), 1)
                if k:
                    dve.wait_ge(S(f"{tag}_hi"), k)
                    dve.tensor_tensor(lo[:, k - 1, :], normed[:, k - 1, :], hi[:, k - 1, :].bitcast(F32),
                                      ALU.subtract).then_inc(S(f"{tag}_lo"), 1)

        def norm_hi(act, tag, n, hi):
            for k in range(n):
                act.wait_ge(S(f"{tag}_scaled"), k + 1)
                act.activation(hi[:, k, :], normed[:, k, :], ACT.Copy).then_inc(S(f"{tag}_hi"), 1)

        def residual_scalar(act, tag, added, first, groups):
            per = 1 if groups == 2 else 2
            for q in range(4):
                for n in range(per):
                    hi_of(act, first + per * q + n + 2) if n == 0 and per == 1 else None
                if per == 2:
                    hi_of(act, first + 2 * q + 2)
                    hi_of(act, first + 2 * q + 3)
                for j in range(2):
                    k = 2 * q + j
                    act.wait_ge(S(added), k + 1)
                    norm_square(act, tag, k, h[:, k, :])

        def residual_vector(dve, added, first, groups):
            per = 1 if groups == 2 else 2
            for q in range(4):
                for n in range(per - 1):
                    lo_of(dve, first + per * q + 2 + n)
                dve.wait_ge(S("w_used"), first + per * (q + 1))
                for j in range(2):
                    k = 2 * q + j
                    dve.tensor_tensor(h[:, k, :], B[2 * (q % 2) + j][:, 0:T], h[:, k, :],
                                      ALU.add).then_inc(S(added), 1)
                lo_of(dve, first + per * q + per + 1)

        def residual_tensor(pe, tag, added, first, n_u, per, spec):
            for q in range(n_u):
                u, grp = first + q, q // per
                if q % per == 0 and grp >= 2:
                    pe.wait_ge(S(added), 2 * (grp - 1))
                pe.wait_ge(S("w_lo_ready"), u + 1)
                s = dict(x0=0, first=True, last=True)
                s.update(spec(q))
                for j in range(2):
                    last = product(pe, u % 2, s["n"], s["k"], P * j, B[2 * (grp % 2) + j], s["xh"], s["xl"],
                                   s["x0"], s["first"], s["last"])
                last.then_inc(S("w_used"), 1)
                if q % per == per - 1 and grp:
                    for k in (2 * grp - 2, 2 * grp - 1):
                        norm_sum(pe, tag, k, KD, B[7])
            for k in (KD - 2, KD - 1):
                norm_sum(pe, tag, k, KD, B[7])

        def scores(b, t):
            return (B[2 * b][:, 0:KEYS_OF_FIRST], B[2 * b + 1][:, 0:T], B[2 * b][0:16, 160:160 + T])[t]

        def rope(dve, bank, dsts, link):
            dve.tensor_tensor(rope_a[NOPE:QH, :], bank[NOPE:QH, 0:T], const[NOPE:QH, C_ROPE:C_ROPE + T], ALU.mult)
            link(dve.tensor_tensor(rope_b[NOPE:QH, :], bank[QH:P, 0:T], const[QH:P, C_ROPE:C_ROPE + T], ALU.mult))
            for dst in dsts:
                last = dve.tensor_tensor(dst, rope_a[NOPE:QH, :], rope_b[NOPE:QH, :], ALU.add)
            link(last)

        w1_v = moe_w1.rearrange("o e (k p) f -> (o e) p k f", p=P)
        w3_v = moe_w3.rearrange("o e (k p) f -> (o e) p k f", p=P)
        w2_v = moe_w2.rearrange("o e (j p) d -> (o e) p j d", p=P)

        ORDER = []
        for c in range(STEPS):
            ORDER += [("w1", c, 0), ("w1", c, 1), ("w3", c, 0), ("w3", c, 1)]
            if c:
                ORDER += [("w2", c - 1, 0), ("w2", c - 1, 1)]
        ORDER += [("w2", STEPS - 1, 0), ("w2", STEPS - 1, 1)]
        assert len(ORDER) == UNITS and UNITS % RAW == 0 and UNITS % SPLIT == 0
        LAST = STEPS - 1

        def moe_load(sp, expert, u):
            kind, c, half = ORDER[u]
            if kind == "w2":
                src = w2_v[bass.ds(expert, 1), :, 4 * c + 2 * half:4 * c + 2 * half + 2, :]
                dst = m_raw[:, u % RAW, :].rearrange("p (k n) -> p k n", k=2)
            else:
                v = w1_v if kind == "w1" else w3_v
                src = v[bass.ds(expert, 1), :, 4 * half:4 * half + 4, c * STEP:(c + 1) * STEP]
                dst = m_raw[:, u % RAW, :].rearrange("p (k n) -> p k n", k=4)
            sp.dma_start(dst, src.rearrange("a p k n -> (a p) k n")).then_inc(S(f"m_landed{u % RAW}"), 16)

        def moe_load_run(sp, m, expert, first=0):
            for u in range(first, UNITS):
                sp.wait_ge(S("m_lo_ready"), m * (2 * UNITS) + 2 * (u - RAW + 1))
                moe_load(sp, expert, u)

        HALF_UNITS = [slice(0, UNIT // 2), slice(UNIT // 2, UNIT)]

        def moe_hi(act, m, u):
            act.wait_ge(S(f"m_landed{u % RAW}"), m * (16 * (UNITS // RAW)) + 16 * (u // RAW + 1))
            act.wait_ge(S("m_used"), m * UNITS + (u + 1))
            for cols in HALF_UNITS:
                act.activation(m_hi[:, u % SPLIT, cols], m_raw[:, u % RAW, cols],
                               ACT.Copy).then_inc(S("m_hi_ready"), 1)

        def moe_lo(dve, m, u):
            for n, cols in enumerate(HALF_UNITS):
                dve.wait_ge(S("m_hi_ready"), m * (2 * UNITS) + (2 * u + n + 1))
                dve.tensor_tensor(m_lo[:, u % SPLIT, cols], m_raw[:, u % RAW, cols],
                                  m_hi[:, u % SPLIT, cols].bitcast(F32), ALU.subtract).then_inc(S("m_lo_ready"), 1)

        H1, H3, GT, Y0, Y1, G0, G1, SM = B
        HALVES = [slice(0, 512), slice(512, 1024)]
        SCATTER = [Y0, Y1, H3, GT]

        def used(m, u):
            return m * UNITS + (u + 1 + SPLIT)

        def gather(pe, m):
            for k in range(KD):
                for t, (_, rows) in enumerate(TOKEN_TILES):
                    for n in range(3):
                        last = pe.matmul((G0, G1)[k // 4][:, (k % 4) * P:(k % 4 + 1) * P],
                                         hf[0:rows, n, t, k * P:(k + 1) * P], pick[0:rows, t, :],
                                         start=t + n == 0, stop=t + n == NT + 1)
            last.then_inc(S("gathered"), 1)
            for t, (t0, rows) in enumerate(TOKEN_TILES):
                pe.transpose(SM.bitcast(BF16)[:, t0:t0 + rows], pick[0:rows, t, :], ident_b[0:rows, 0:rows])
            for t, (_, rows) in enumerate(TOKEN_TILES):
                for n in range(3):
                    last = pe.matmul(SM[:, 384:384 + N_EXPERTS], pick[0:rows, t, :],
                                     gate_part[0:rows, n, t, :], start=t + n == 0, stop=t + n == NT + 1)
            last.then_inc(S("pickT_done"), 1)

        def transpose_step(pe, m, c):
            pe.wait_ge(S("gated_ready"), m * STEPS + (c + 1))
            for j in range(4):
                last = pe.transpose(GT[:, j * P:(j + 1) * P], gated[:, j * P:(j + 1) * P], ident)
            last.then_inc(S("gt_done"), 1)

        def scatter(pe, m):
            for n in range(2):
                pe.wait_ge(S("y_ready"), 2 * m + (n + 1))
                for t, (t0, rows) in enumerate(TOKEN_TILES):
                    i = NT * n + t
                    if i >= len(SCATTER):
                        pe.wait_ge(S("acc_added"), 2 * NT * m + (i - len(SCATTER) + 2))
                    bank = SCATTER[i % len(SCATTER)]
                    pe.matmul(bank[0:rows, :], pickT[:, t0:t0 + rows], y_hi[:, HALVES[n]], start=True, stop=False)
                    pe.matmul(bank[0:rows, :], pickT[:, t0:t0 + rows], y_lo[:, HALVES[n]], start=False,
                              stop=True).then_inc(S("scattered"), 1)

        def run_tensor(pe, m):
            for u, (kind, c, half) in enumerate(ORDER):
                if u == 0:
                    pe.wait_ge(S("xe_ready"), m + 1)
                if kind == "w1" and half == 0:
                    pe.wait_ge(S("h1_free"), m * STEPS + (c + 1))
                if kind == "w3" and half == 0 and c:
                    transpose_step(pe, m, c - 1)
                if kind == "w3" and half == 0 and c == 0:
                    pe.wait_ge(S("acc_added"), 2 * NT * m + 1)
                if u == UNITS - 3:
                    transpose_step(pe, m, LAST)
                if kind == "w2" and half == 0:
                    pe.wait_ge(S("gt_ready"), m * STEPS + (c + 1))
                n = 2 if kind == "w2" else 4
                wh, wl = (w[:, u % SPLIT, :].rearrange("p (k n) -> p k n", k=n) for w in (m_hi, m_lo))
                for kk in range(n):
                    if kk % (n // 2) == 0:
                        pe.wait_ge(S("m_lo_ready"), m * (2 * UNITS) + (2 * u + kk // (n // 2) + 1))
                    k = n * half + kk
                    if kind == "w2":
                        for cols, bank in zip(HALVES, (Y0, Y1)):
                            last = moving(pe, bank, gt_hi[:, c % 2, k, :], gt_lo[:, c % 2, k, :], wh[:, kk, cols],
                                          wl[:, kk, cols], c == 0 and k == 0, c == LAST and k == 3)
                    else:
                        last = moving(pe, H1 if kind == "w1" else H3, xe_hi[:, k, :], xe_lo[:, k, :],
                                      wh[:, kk, :], wl[:, kk, :], k == 0, k == KD - 1)
                last.then_inc(S("m_used"), 1)
            pe.wait_ge(S("pick_ready"), m + 2)
            pe.wait_ge(S("pickT_copied"), m + 1)
            pe.wait_ge(S("gates_copied"), m + 1)
            gather(pe, m + 1)
            scatter(pe, m)

        def moving(pe, o, xh, xl, wh, wl, first, last):
            pe.matmul(o, xh, wh, start=first, stop=False)
            pe.matmul(o, xh, wl, start=False, stop=False)
            return pe.matmul(o, xl, wh, start=False, stop=last)

        def gt_hi_copy(act, m, c):
            act.wait_ge(S("gt_done"), m * STEPS + (c + 1))
            act.activation(gt_hi[:, c % 2, :, :], GT.rearrange("p (j n) -> p j n", j=4),
                           ACT.Copy).then_inc(S("gt_hi_ready"), 1)

        def xe_hi_copy(act, m):
            act.wait_ge(S("gathered"), m + 1)
            for i, bank in enumerate((G0, G1)):
                act.activation(xe_hi[:, 4 * i:4 * i + 4, :], bank.rearrange("p (j n) -> p j n", j=4),
                               ACT.Copy).then_inc(S("xe_hi_ready"), 1)

        def ahead(m, u, following):
            if u + SPLIT < UNITS:
                return m, u + SPLIT
            return (m + 1, u + SPLIT - UNITS) if following else None

        def run_scalar(act, m, leading, following):
            if leading:
                for u in range(SPLIT):
                    moe_hi(act, m, u)
            for u, (kind, c, half) in enumerate(ORDER):
                nxt = ahead(m, u, following)
                if u == UNITS - 3:
                    gt_hi_copy(act, m, LAST)
                if nxt and u < UNITS - 1:
                    moe_hi(act, *nxt)
                if kind == "w1" and half == 1:
                    if c == 1:
                        act.wait_ge(S("pickT_done"), m + 1)
                        act.activation(pickT[:, :], SM.bitcast(BF16)[:, 0:T], ACT.Copy).then_inc(S("pickT_copied"), 1)
                    act.wait_ge(S("m_used"), used(m, u))
                    if c:
                        act.wait_ge(S("gated_ready"), m * STEPS + c)
                    act.activation(silu_e[:, :], H1, ACT.Silu).then_inc(S("h1_free"), 1)
                    if c:
                        gt_hi_copy(act, m, c - 1)
            for n in range(2):
                act.wait_ge(S("y_f32_ready"), 2 * m + (n + 1))
                act.activation(y_hi[:, HALVES[n]], y_f32[:, HALVES[n]], ACT.Copy).then_inc(S("y_hi_ready"), 1)
            xe_hi_copy(act, m + 1)
            if following:
                moe_hi(act, *ahead(m, UNITS - 1, True))

        def gt_lo_copy(dve, m, c):
            dve.wait_ge(S("gt_hi_ready"), m * STEPS + (c + 1))
            dve.tensor_tensor(gt_lo[:, c % 2, :, :], GT.rearrange("p (j n) -> p j n", j=4),
                              gt_hi[:, c % 2, :, :].bitcast(F32), ALU.subtract).then_inc(S("gt_ready"), 1)

        def xe_lo_copy(dve, m):
            for i, bank in enumerate((G0, G1)):
                dve.wait_ge(S("xe_hi_ready"), 2 * m + (i + 1))
                last = dve.tensor_tensor(xe_lo[:, 4 * i:4 * i + 4, :], bank.rearrange("p (j n) -> p j n", j=4),
                                         xe_hi[:, 4 * i:4 * i + 4, :].bitcast(F32), ALU.subtract)
            last.then_inc(S("xe_ready"), 1)

        def pick_run(dve, m):
            for t in range(NT):
                last = dve.tensor_scalar(pick[:, t, :], const[:, C_IOTA:C_IOTA + P],
                                         place[:, t, bass.ds(m, 1)], None, ALU.is_equal)
            last.then_inc(S("pick_ready"), 1)

        def run_vector(dve, m, expert, leading, following):
            if leading:
                for u in range(SPLIT):
                    moe_lo(dve, m, u)
            for u, (kind, c, half) in enumerate(ORDER):
                nxt = ahead(m, u, following)
                if kind == "w3" and half == 1:
                    dve.wait_ge(S("m_used"), used(m, u))
                    dve.wait_ge(S("h1_free"), m * STEPS + (c + 2))
                    if c:
                        dve.wait_ge(S("gt_hi_ready"), m * STEPS + c)
                    dve.tensor_tensor(gated[:, :], H3, silu_e[:, :], ALU.mult).then_inc(S("gated_ready"), 1)
                if u == UNITS - 3:
                    gt_lo_copy(dve, m, LAST)
                if nxt and u < UNITS - 1:
                    moe_lo(dve, *nxt)
                if kind == "w1" and half == 1 and c:
                    gt_lo_copy(dve, m, c - 1)
                    if c == 1:
                        dve.wait_ge(S("pickT_copied"), m + 1)
                        dve.tensor_copy(g_slot[:, 0:1], SM[:, bass.ds(expert + 384, 1)])\
                            .then_inc(S("gates_copied"), 1)
                        pick_run(dve, m + 1)
            dve.wait_ge(S("m_used"), used(m, UNITS - 1))
            dve.wait_ge(S("gates_copied"), m + 1)
            for n, bank in enumerate((Y0, Y1)):
                dve.tensor_scalar(y_f32[:, HALVES[n]], bank, g_slot[:, 0:1], None,
                                  ALU.mult).then_inc(S("y_f32_ready"), 1)
            for n in range(2):
                dve.wait_ge(S("y_hi_ready"), 2 * m + (n + 1))
                dve.tensor_tensor(y_lo[:, HALVES[n]], y_f32[:, HALVES[n]], y_hi[:, HALVES[n]].bitcast(F32),
                                  ALU.subtract).then_inc(S("y_ready"), 1)
            xe_lo_copy(dve, m + 1)
            for n in range(2):
                for t, (_, rows) in enumerate(TOKEN_TILES):
                    i = NT * n + t
                    dve.wait_ge(S("scattered"), 2 * NT * m + (i + 1))
                    last = dve.tensor_tensor(acc[0:rows, t, HALVES[n]], SCATTER[i % len(SCATTER)][0:rows, :],
                                             acc[0:rows, t, HALVES[n]], ALU.add)
                    last.then_inc(S("acc_added"), 1)
            if following:
                moe_lo(dve, *ahead(m, UNITS - 1, True))

        def overflow(eng, body):
            eng.wait_ge(S("count_ready"), 1)
            most = eng.value_load(count_i[0:1, 0:1], min_val=0, max_val=T)
            with eng.If(most > P):
                with eng.Fori(1, PASSES) as again:
                    with eng.Fori(0, N_EXPERTS) as e:
                        body(again * N_EXPERTS + e, e)

        block = ctx.enter_context(nc.Block())

        @block.sync
        def _(sp):
            sp.dma_start(x_rows[0:N_META, 0, :], meta_tokens).then_inc(S("x_landed"), 16)
            sp.dma_start(x_rows[N_META:P, 0, :], x[0, 0:P - N_META, :]).then_inc(S("x_landed"), 16)
            sp.dma_start(x_rows[:, 1, :], x[0, P - N_META:2 * P - N_META, :]).then_inc(S("x_landed"), 16)
            sp.dma_start(x_rows[0:N_META, 2, :], x[0, 2 * P - N_META:SEQ, :]).then_inc(S("x_landed"), 16)
            for u in range(U_X, U_G):
                load_256(sp, u, u % 2, w_in_v, (D + 256 * u) % (2 * D))
            g_raw = raw[:, U_G % 2, 0:2048].rearrange("p (w n c) -> p w n c", w=2, n=N_BLOCKS)
            dma_unit(sp, U_G, U_G % 2, [(g_raw[:, 0], rnn_w_a.rearrange("o n c d -> (o c) n d")),
                                        (g_raw[:, 1], rnn_w_i.rearrange("o n c d -> (o c) n d"))])
            for q in range(4):
                load_256(sp, U_O + q, (U_O + q) % 2, w_out_v, 256 * q)
            with sp.Fori(0, KF // 2) as i:
                load_256(sp, U_F + 2 * i, U_F % 2, f1_v, 256 * i)
                load_256(sp, U_F + 1 + 2 * i, (U_F + 1) % 2, f3_v, 256 * i)
            for q in range(8):
                u, half = U_W2 + q, q % 2
                rows = f2_v[half * (D_FF // 2):(half + 1) * (D_FF // 2), :]
                dma_unit(sp, u, u % 2, [(raw_v(u % 2, 11 * 256, 11), src_cols(rows, 256 * (q // 2), 256))])
            dma_unit(sp, U_KV, U_KV % 2, [(raw_v(U_KV % 2, 8 * 288, 8), src_cols(kv_w_down, 0, 288))])
            dma_unit(sp, U_Q, U_Q % 2, [(raw_v(U_Q % 2, 8 * Q_LORA, 8), src_cols(qd_v, 0, Q_LORA))])

            def load_heads(g):
                u = U_H + g
                dma_unit(sp, u, u % 2,
                         [(raw_v(u % 2, 1024, 2), src_cols(kv_w_up, 512 * g, 512)),
                          (raw[:, u % 2, 1024:1024 + 12 * QH].rearrange("p (k n) -> p k n", k=KQ),
                           src_cols(qu_v, 4 * QH * g, 4 * QH))])

            load_heads(0)
            load_heads(1)
            sp.wait_ge(S("w_used"), U_KV)
            for u in range(3):
                moe_load(sp, 0, u)
            load_heads(2)
            load_heads(3)
            for u in range(3, RAW - 1):
                moe_load(sp, 0, u)
            for q in range(4):
                load_256(sp, U_AO + q, (U_AO + q) % 2, ao_v, 256 * q)
                if q == 1:
                    sp.wait_ge(S("q_ready"), HEADS)
                    moe_load(sp, 0, RAW - 1)
            sp.wait_ge(S("w_used"), n_units)
            sp.dma_start(g_final[:, :], norm_final.partition_broadcast(P)).then_inc(S("g_final_landed"), 16)
            moe_load_run(sp, 0, 0, RAW)
            with sp.Fori(1, N_EXPERTS) as m:
                moe_load_run(sp, m, m)
            overflow(sp, lambda m, e: moe_load_run(sp, m, e))
            for t, (t0, rows) in enumerate(TOKEN_TILES):
                skip = N_META if t == 0 else 0
                sp.wait_ge(S("y_out_ready"), t + 1)
                sp.dma_start(out[0, t0 + skip - N_META:t0 + rows - N_META, :],
                             y_out[skip:rows, t, :]).then_inc(S("out_landed"), 16)
            sp.wait_ge(S("out_landed"), 16 * NT)

        @block.gpsimd
        def _(pool):
            pool.memset(ones[:, :], 1.0)
            pool.memset(eps, EPS)
            pool.memset(x_pad[:, :, 0:CONV - 1], 0.0).then_inc(S("pool_set"), 1)
            pool.wait_ge(S("z_gain_ready"), 1)
            for k in range(N_BLOCKS):
                pool.wait_ge(S("gates_done"), 2 * k + 2)
                pool.tensor_scalar(tanh_z[:, k, :], gate_r[:, k, :], sp_t[:, 7, k:k + 1], None,
                                   ALU.mult).then_inc(S("z_ready"), 1)
                pool.tensor_tensor(gate_i[:, k, :], gate_i[:, k, :], x_conv[:, k, :],
                                   ALU.mult).then_inc(S("gated_x"), 1)
            pool.wait_ge(S("w_used"), U_H)
            pool.memset(prob0[:, :, :], 0.0).then_inc(S("prob0_cleared"), 1)
            for j in range(HEADS):
                pool.wait_ge(S("p_inv_ready"), j + 1)
                b = j % 2
                pool.tensor_scalar(prob0[:, b, 0:KEYS_OF_FIRST], prob0[:, b, 0:KEYS_OF_FIRST],
                                   p_inv[:, b, 0:1], None, ALU.mult)
                pool.tensor_scalar(prob2[0:16, b, :], prob2[0:16, b, :], p_inv[0:16, b, 2:3], None,
                                   ALU.mult).then_inc(S("prob_ready"), 1)

        @block.scalar
        def _(act):
            act.sem_inc(S("silu_ready"), 1)
            act.sem_inc(S("h1_free"), 1)
            act.dma_start(const[:, :], consts).then_inc(S("const_landed"), 16)
            row = 0
            for src in (norm_mix.rearrange("l (k p) -> (l k) p", p=P), norm_ffn.rearrange("l (k p) -> (l k) p", p=P),
                        kv_norm_src.rearrange("(k p) -> k p", p=P),
                        rnn_conv_w.rearrange("o w (k p) -> (o w k) p", p=P),
                        rnn_conv_b.rearrange("o (k p) -> (o k) p", p=P), rnn_b_a.rearrange("o (k p) -> (o k) p", p=P),
                        rnn_b_i.rearrange("o (k p) -> (o k) p", p=P), rnn_lambda.rearrange("o (k p) -> (o k) p", p=P),
                        q_latent_norm.rearrange("o (k p) -> (o k) p", p=P),
                        kv_latent_norm.rearrange("(k p) -> k p", p=P)):
                n = src.shape[0]
                act.dma_start(p_rows[row:row + n, :], src).then_inc(S("params_landed"), 16)
                row += n
            act.dma_start(router[:, :, :], moe_router.rearrange("o (k p) e -> (o p) k e", p=P))\
                .then_inc(S("router_landed"), 16)
            hi_of(act, U_X)
            for k in range(KD):
                act.wait_ge(S("h0_ready"), k + 1)
                norm_square(act, "n0", k, h[:, k, :])
            hi_of(act, U_X + 1)
            act.wait_ge(S("pool_set"), 1)
            norm_std(act, "n0", KD, B[0])
            norm_hi(act, "n0", KD, a_hi)
            act.wait_ge(S("neg_abs_ready"), 1)
            act.activation(sp_t[:, 1, :], sp_t[:, 0, :], ACT.Exp).then_inc(S("exp_lam"), 1)
            for u in range(U_X, U_Y):
                hi_of(act, u + 2)
            for u in range(U_Y, U_G):
                act.wait_ge(S("w_used"), u + 1)
                for j in range(2):
                    k = 2 * (u - U_Y) + j
                    last = act.activation(y_gate[:, k, :], B[2 * (u % 2) + j][:, 0:T], ACT.Gelu_apprx_tanh)
                last.then_inc(S("y_gate_ready"), 1)
                hi_of(act, u + 2)
                for j in range(2):
                    k = 2 * (u - U_Y) + j
                    act.wait_ge(S("conv_ready"), k + 1)
                    act.activation(b_hi[:, k, :], x_conv[:, k, :], ACT.Copy).then_inc(S("xc_hi_ready"), 1)
            for k in range(N_BLOCKS):
                for g, (bias, dst) in enumerate((("b_a", gate_r), ("b_i", gate_i))):
                    act.wait_ge(S("gate_psum"), 2 * k + g + 1)
                    act.activation(dst[:, k, :], B[(2 * k + g) % 8][:, 0:T], ACT.Sigmoid,
                                   bias=prm(bias, k)).then_inc(S("gates_done"), 1)
            for part in range(2):
                ks = slice(4 * part, 4 * part + 4)
                act.wait_ge(S("z_ready"), 4 * part + 4)
                act.activation(decay[:, ks, :], tanh_z[:, ks, :], ACT.Exp, scale=-1.0)
                act.activation(gate_r[:, ks, :], tanh_z[:, ks, :], ACT.Exp, scale=-2.0).then_inc(S("decays"), 1)
                act.wait_ge(S("decays"), part + 1)
                act.activation(tanh_z[:, ks, :], tanh_z[:, ks, :], ACT.Tanh).then_inc(S("tanh_ready"), 1)
            hi_of(act, U_G + 2)
            for part in range(2):
                ks = slice(4 * part, 4 * part + 4)
                act.wait_ge(S("one_less_sq"), part + 1)
                act.activation(tanh_z[:, ks, :], gate_r[:, ks, :], ACT.Sqrt).then_inc(S("mult_ready"), 1)
            for k in range(KD):
                act.wait_ge(S("mixed"), k + 1)
                act.activation(a_hi[:, k, :], gate_r[:, k, :], ACT.Copy).then_inc(S("mixed_hi"), 1)
            residual_scalar(act, "n1", "o_added", U_O, 2)
            norm_std(act, "n1", KD, B[7])
            norm_hi(act, "n1", KD, a_hi)

            def up_step(i):
                act.wait_ge(S("w_used"), U_F + 1 + 2 * i)
                for j in range(2):
                    last = act.activation(silu[:, j, :], B[j][:, 0:T], ACT.Silu)
                last.then_inc(S("silu_ready"), 1)

            def up_hi(i):
                for j in range(2):
                    act.wait_ge(S("g_ready"), 2 * i + (j + 3))
                    act.activation(g_hi[:, bass.ds(2 * i + j, 1), :], g_f32[:, j:j + 1, :],
                                   ACT.Copy).then_inc(S("g_hi_ready"), 1)

            with act.Fori(0, KF // 2 - 1) as i:
                up_step(i)
                split_hi(act, U_F + 2 + 2 * i, U_F % 2, 2048, units.arrived[U_F + 2] + 16 * i)
                split_hi(act, U_F + 3 + 2 * i, (U_F + 1) % 2, 2048, units.arrived[U_F + 3] + 16 * i)
                up_hi(i)
            up_step(KF // 2 - 1)
            hi_of(act, U_W2)
            hi_of(act, U_W2 + 1)
            up_hi(KF // 2 - 1)
            residual_scalar(act, "n2", "w2_added", U_W2, 4)
            norm_std(act, "n2", KD, B[7])
            norm_hi(act, "n2", KD, a_hi)
            norm_hi(act, "n2b", KD, b_hi)
            for k in range(KC):
                act.wait_ge(S("latent_kv_ready"), k + 1)
                norm_square(act, "nk", k, latent_kv[:, k, :])
            for b in range(2):
                act.activation(q_head[96:96 + N_CHUNKS, b, :], const[96:96 + N_CHUNKS, C_QMASK:C_QMASK + T], ACT.Copy)
                last = act.activation(k_head[96:96 + N_CHUNKS, b, :], const[96:96 + N_CHUNKS, C_KMASK:C_KMASK + T],
                                      ACT.Copy)
            last.then_inc(S("mask_rows"), 1)
            hi_of(act, U_H)
            act.wait_ge(S("nk_summed"), KC)
            norm_std(act, "nk", KC, B[7])
            norm_hi(act, "nk", KC, c_hi)
            for k in range(KQ):
                act.wait_ge(S("latent_q_ready"), k + 1)
                norm_square(act, "nq", k, latent_q[:, k, :])
            act.wait_ge(S("nk_inv"), 1)
            norm_std(act, "nq", KQ, B[6])
            norm_hi(act, "nq", KQ, cq_hi)
            for s in range(HEADS + 3):
                if s < HEADS:
                    b = s % 2
                    if s >= 2:
                        act.wait_ge(S("scored"), s - 1)
                    act.wait_ge(S("kq_psum"), 2 * s + 1)
                    act.activation(k_head[0:NOPE, b, :], B[4][0:NOPE, 0:T], ACT.Copy)
                    act.wait_ge(S("kq_psum"), 2 * s + 2)
                    act.activation(q_head[0:NOPE, b, :], B[5][0:NOPE, 0:T], ACT.Copy).then_inc(S("kq_ready"), 1)
                if s >= 4 and s % 2 == 0:
                    k = (s - 4) // 2
                    act.wait_ge(S("weighted"), s - 2)
                    act.activation(a_hi[:, k, :], B[7][:, 0:T], ACT.Copy).then_inc(S("o_hi_ready"), 1)
                if 1 <= s <= HEADS:
                    j, b = s - 1, (s - 1) % 2
                    act.wait_ge(S("bias_ready"), j + 1)
                    if j == 0:
                        act.wait_ge(S("prob0_cleared"), 1)
                    if j >= 2:
                        act.wait_ge(S("p_transposed"), j - 1)
                    for t, (_, rows) in enumerate(TOKEN_TILES):
                        dst = (prob0[:, b, 0:KEYS_OF_FIRST], prob1[:, b, :], prob2[0:rows, b, :])[t]
                        last = act.activation(dst, scores(b, t), ACT.Exp, bias=bias_e[0:rows, b, t:t + 1],
                                              scale=SCALE, accum_out=p_sum[0:rows, b, t:t + 1])
                    last.then_inc(S("exp_done"), 1)
                if 2 <= s < HEADS + 2:
                    j, b = s - 2, s % 2
                    act.wait_ge(S("p_transposed"), j + 1)
                    if j >= 2:
                        act.wait_ge(S("weighted"), j - 1)
                    act.activation(probT[:, b, :], B[6][:, 0:T + 208], ACT.Copy)
                    act.activation(probT2[0:16, b, :], B[7][0:16, T:T + 80], ACT.Copy).then_inc(S("probT_ready"), 1)
                if s % 4 == 1:
                    hi_of(act, U_H + s // 4 + 1)
            residual_scalar(act, "n3", "ao_added", U_AO, 2)
            norm_std(act, "n3", KD, B[7])
            for i in range(2 * NT):
                t, rows = i // 2, TOKEN_TILES[i // 2][1]
                act.wait_ge(S("h_rows"), i + 1)
                act.activation(acc[0:rows, t, HALVES[i % 2]], B[i][0:rows, :], ACT.Copy).then_inc(S("acc_set"), 1)
            for i in range(2 * NT):
                t, rows = i // 2, TOKEN_TILES[i // 2][1]
                act.wait_ge(S("hf_rows"), i + 1)
                act.activation(hf[0:rows, 0, t, HALVES[i % 2]], B[i][0:rows, :], ACT.Copy)\
                    .then_inc(S("hf_0_ready"), 1)
                act.wait_ge(S("hf_rest_ready"), i + 1)
                act.activation(hf[0:rows, 1, t, HALVES[i % 2]], rest[0:rows, i % 2, :], ACT.Copy)\
                    .then_inc(S("hf_1_ready"), 1)
            act.activation(ident_b[:, :], ident, ACT.Copy).then_inc(S("ident_b_ready"), 1)
            act.wait_ge(S("r_shifted"), 1)
            act.activation(r_exp[:, :, :], r_exp[:, :, :], ACT.Exp).then_inc(S("r_exp_ready"), 1)
            act.wait_ge(S("w_used"), n_units)
            xe_hi_copy(act, 0)
            for u in range(SPLIT):
                moe_hi(act, 0, u)
            with act.Fori(0, N_EXPERTS - 1) as m:
                run_scalar(act, m, False, True)
            run_scalar(act, N_EXPERTS - 1, False, False)
            overflow(act, lambda m, e: run_scalar(act, m, True, False))
            act.wait_ge(S("acc_done"), 1)
            for t, (_, rows) in enumerate(TOKEN_TILES):
                last = act.activation(y_out[0:rows, t, :], acc[0:rows, t, :], ACT.Square,
                                      accum_out=ss[0:rows, 0, t:t + 1])
            last.then_inc(S("ss_ready"), 1)
            act.wait_ge(S("ss_ready"), 1)
            act.activation(ss[:, 1, :], ss[:, 0, :], ACT.Sqrt, bias=eps, scale=1.0 / D).then_inc(S("last_std"), 1)

        @block.vector
        def _(dve):
            own = [0]

            def link(ins):
                own[0] += 1
                ins.then_inc(S("dve_own"), 1)
                dve.wait_ge(S("dve_own"), own[0])

            dve.sem_inc(S("acc_added"), 1)
            dve.sem_inc(S("g_ready"), 2)
            dve.sem_inc(S("g_lo_ready"), 1)
            for k in range(KD):
                dve.wait_ge(S("x_transposed"), k + 1)
                dve.tensor_copy(h[:, k, :], B[k][:, 0:T]).then_inc(S("h0_ready"), 1)
            dve.wait_ge(S("params_transposed"), 1)
            link(dve.tensor_copy(params[:, :], B[1][:, 384:384 + N_PARAMS]))
            lo_of(dve, U_X)
            lo_of(dve, U_X + 1)
            norm_inv(dve, "n0")
            norm_scale(dve, "n0", KD, h, lambda k: prm("norm_mix", k), a_hi, a_lo)
            dve.wait_ge(S("n0_lo"), KD)
            lam = params[:, PCOL["lam"]:PCOL["lam"] + N_BLOCKS]
            link(dve.tensor_scalar(sp_t[:, 2, :], lam, -1.0, None, ALU.mult))
            link(dve.tensor_tensor(sp_t[:, 0, :], sp_t[:, 2, :], lam, ALU.min))
            dve.sem_inc(S("neg_abs_ready"), 1)
            dve.tensor_scalar(sp_t[:, 2, :], sp_t[:, 2, :], 0.0, None, ALU.max)
            dve.wait_ge(S("exp_lam"), 1)
            link(dve.tensor_scalar(sp_t[:, 3, :], sp_t[:, 1, :], 2.0, None, ALU.add))
            link(dve.reciprocal(sp_t[:, 4, :], sp_t[:, 3, :]))
            link(dve.tensor_tensor(sp_t[:, 3, :], sp_t[:, 1, :], sp_t[:, 4, :], ALU.mult))
            link(dve.tensor_tensor(sp_t[:, 4, :], sp_t[:, 3, :], sp_t[:, 3, :], ALU.mult))
            link(dve.tensor_scalar(sp_t[:, 5, :], sp_t[:, 4, :], 1.0 / 17, None, ALU.mult))
            for n in range(7, 0, -1):
                link(dve.scalar_tensor_tensor(sp_t[:, 5, :], sp_t[:, 5, :], 1.0 / (2 * n + 1), sp_t[:, 4, :],
                                              ALU.add, ALU.mult))
            link(dve.scalar_tensor_tensor(sp_t[:, 5, :], sp_t[:, 5, :], 1.0, sp_t[:, 3, :], ALU.add, ALU.mult))
            link(dve.scalar_tensor_tensor(sp_t[:, 6, :], sp_t[:, 5, :], 2.0, sp_t[:, 2, :], ALU.mult, ALU.add))
            dve.tensor_scalar(sp_t[:, 7, :], sp_t[:, 6, :], LRU_C, None, ALU.mult).then_inc(S("z_gain_ready"), 1)
            for u in range(U_X, U_Y):
                dve.wait_ge(S("w_used"), u + 1)
                if u == U_X:
                    dve.wait_ge(S("pool_set"), 1)
                for j in range(2):
                    last = dve.tensor_copy(x_pad[:, 2 * u + j, CONV - 1:], B[2 * (u % 2) + j][:, 0:T])
                last.then_inc(S("x_evacuated"), 1)
                lo_of(dve, u + 2)
            dve.wait_ge(S("x_evacuated"), 4)
            for u in range(U_Y, U_G):
                for w in range(CONV):
                    for j in range(2):
                        k = 2 * (u - U_Y) + j
                        tap = x_pad[:, k, w:w + T]
                        if w == 0:
                            last = dve.tensor_scalar(x_conv[:, k, :], tap, prm("conv_w", k), prm("conv_b", k),
                                                     ALU.mult, ALU.add)
                        else:
                            last = dve.scalar_tensor_tensor(x_conv[:, k, :], tap, prm("conv_w", 8 * w + k),
                                                            x_conv[:, k, :], ALU.mult, ALU.add)
                        if w == CONV - 1:
                            last.then_inc(S("conv_ready"), 1)
                    if w < CONV - 1:
                        link(last)
                lo_of(dve, u + 2)
                for j in range(2):
                    k = 2 * (u - U_Y) + j
                    dve.wait_ge(S("xc_hi_ready"), k + 1)
                    dve.tensor_tensor(b_lo[:, k, :], x_conv[:, k, :], b_hi[:, k, :].bitcast(F32),
                                      ALU.subtract).then_inc(S("xc_lo_ready"), 1)
            for part in range(2):
                ks = slice(4 * part, 4 * part + 4)
                dve.wait_ge(S("tanh_ready"), part + 1)
                dve.scalar_tensor_tensor(gate_r[:, ks, :], gate_r[:, ks, :], 1.0, tanh_z[:, ks, :], ALU.add,
                                         ALU.mult).then_inc(S("one_less_sq"), 1)
            lo_of(dve, U_G + 2)
            for part in range(2):
                ks = slice(4 * part, 4 * part + 4)
                dve.wait_ge(S("mult_ready"), part + 1)
                dve.wait_ge(S("gated_x"), 4 * part + 4)
                link(dve.tensor_tensor(gate_i[:, ks, :], tanh_z[:, ks, :], gate_i[:, ks, :], ALU.mult))
                for k in range(4 * part, 4 * part + 4):
                    last = dve.tensor_tensor_scan(x_conv[:, k, :], decay[:, k, :], gate_i[:, k, :], 0.0,
                                                  ALU.mult, ALU.add)
                link(last)
                dve.wait_ge(S("y_gate_ready"), 4)
                for k in range(4 * part, 4 * part + 4):
                    dve.tensor_tensor(gate_r[:, k, :], x_conv[:, k, :], y_gate[:, k, :],
                                      ALU.mult).then_inc(S("mixed"), 1)
                for k in range(4 * part, 4 * part + 4):
                    dve.wait_ge(S("mixed_hi"), k + 1)
                    dve.tensor_tensor(a_lo[:, k, :], gate_r[:, k, :], a_hi[:, k, :].bitcast(F32),
                                      ALU.subtract).then_inc(S("mixed_lo"), 1)
            residual_vector(dve, "o_added", U_O, 2)
            norm_inv(dve, "n1")
            norm_scale(dve, "n1", KD, h, lambda k: prm("norm_ffn", k), a_hi, a_lo)

            def up_product(i):
                dve.wait_ge(S("w_used"), U_F + 2 + 2 * i)
                dve.wait_ge(S("silu_ready"), i + 2)
                dve.wait_ge(S("g_lo_ready"), i + 1)
                for j in range(2):
                    dve.tensor_tensor(g_f32[:, j, :], B[2 + j][:, 0:T], silu[:, j, :],
                                      ALU.mult).then_inc(S("g_ready"), 1)

            def up_lo(i):
                for j in range(2):
                    dve.wait_ge(S("g_hi_ready"), 2 * i + (j + 1))
                    last = dve.tensor_tensor(g_lo[:, bass.ds(2 * i + j, 1), :], g_f32[:, j:j + 1, :],
                                             g_hi[:, bass.ds(2 * i + j, 1), :].bitcast(F32), ALU.subtract)
                last.then_inc(S("g_lo_ready"), 1)

            with dve.Fori(0, KF // 2 - 1) as i:
                split_lo(dve, U_F + 2 + 2 * i, U_F % 2, 2048)
                up_product(i)
                split_lo(dve, U_F + 3 + 2 * i, (U_F + 1) % 2, 2048)
                up_lo(i)
            lo_of(dve, U_W2)
            up_product(KF // 2 - 1)
            lo_of(dve, U_W2 + 1)
            up_lo(KF // 2 - 1)
            residual_vector(dve, "w2_added", U_W2, 4)
            norm_inv(dve, "n2")
            norm_scale(dve, "n2", KD, h, lambda k: prm("kv_src", k), a_hi, a_lo)
            norm_scale(dve, "n2b", KD, h, lambda k: prm("norm_mix", KD + k), b_hi, b_lo)
            dve.wait_ge(S("w_used"), U_KV + 1)
            for k in range(KC):
                dve.tensor_copy(latent_kv[:, k, :], B[k][:, 0:T]).then_inc(S("latent_kv_ready"), 1)
            rope(dve, B[2], [k_head[NOPE:QH, 0, :], k_head[NOPE:QH, 1, :]], link)
            dve.memset(n_max[:, :, :], 0.0)
            link(dve.memset(p_sum[:, :, :], 1.0))
            lo_of(dve, U_H)
            norm_inv(dve, "nk")
            norm_scale(dve, "nk", KC, latent_kv, lambda k: prm("kv_lat", k), c_hi, c_lo)
            dve.wait_ge(S("w_used"), U_Q + 1)
            for k in range(KQ):
                dve.tensor_copy(latent_q[:, k, :], B[3 + k][:, 0:T]).then_inc(S("latent_q_ready"), 1)
            norm_inv(dve, "nq")
            norm_scale(dve, "nq", KQ, latent_q, lambda k: prm("q_lat", k), cq_hi, cq_lo)
            for s in range(HEADS + 3):
                if s < HEADS and s % 4 == 0:
                    g = s // 4
                    dve.wait_ge(S("v_psum"), g + 1)
                    dve.tensor_copy(v_sb[:, g % 2, 0:2, :], B[4].rearrange("p (t n) -> p t n", t=2))
                    dve.tensor_copy(v_sb[0:16, g % 2, 2, :], B[5][0:16, 0:256]).then_inc(S("v_ready"), 1)
                if 2 <= s < HEADS + 2:
                    j, b = s - 2, s % 2
                    dve.wait_ge(S("exp_done"), j + 1)
                    if j >= 2:
                        dve.wait_ge(S("prob_ready"), j - 1)
                    dve.reciprocal(p_inv[:, b, 0:NT], p_sum[:, b, 0:NT]).then_inc(S("p_inv_ready"), 1)
                    dve.wait_ge(S("p_inv_ready"), j + 1)
                    dve.tensor_scalar(prob1[:, b, :], prob1[:, b, :], p_inv[:, b, 1:2], None,
                                      ALU.mult).then_inc(S("prob1_ready"), 1)
                if s < HEADS:
                    if s >= 2:
                        dve.wait_ge(S("scored"), s - 1)
                    dve.wait_ge(S("kq_psum"), 2 * s + 2)
                    rope(dve, B[5], [q_head[NOPE:QH, s % 2, :]], link)
                    dve.sem_inc(S("q_ready"), 1)
                if s >= 4 and s % 2 == 0:
                    k = (s - 4) // 2
                    dve.wait_ge(S("o_hi_ready"), k + 1)
                    dve.tensor_tensor(a_lo[:, k, :], B[7][:, 0:T], a_hi[:, k, :].bitcast(F32),
                                      ALU.subtract).then_inc(S("o_lo_ready"), 1)
                if 1 <= s <= HEADS:
                    j, b = s - 1, (s - 1) % 2
                    dve.wait_ge(S("scored"), j + 1)
                    for t, (_, rows) in enumerate(TOKEN_TILES):
                        last = dve.tensor_reduce(n_max[0:rows, b, t:t + 1], scores(b, t), AX.X, ALU.max)
                    link(last)
                    if j >= 2:
                        dve.wait_ge(S("exp_done"), j - 1)
                    dve.tensor_scalar(bias_e[:, b, 0:NT], n_max[:, b, 0:NT], -SCALE, None,
                                      ALU.mult).then_inc(S("bias_ready"), 1)
                if s % 4 == 1:
                    lo_of(dve, U_H + s // 4 + 1)
            residual_vector(dve, "ao_added", U_AO, 2)
            norm_inv(dve, "n3")
            for k in range(KD):
                dve.scalar_tensor_tensor(normed[:, k, :], h[:, k, :], prm("norm_ffn", KD + k), rstd[:, :],
                                         ALU.mult, ALU.mult).then_inc(S("n3_scaled"), 1)
            for i in range(2 * NT):
                t, rows = i // 2, TOKEN_TILES[i // 2][1]
                dve.wait_ge(S("hf_0_ready"), i + 1)
                if i >= 2:
                    dve.wait_ge(S("hf_2_ready"), i - 1)
                dve.tensor_tensor(rest[0:rows, i % 2, :], B[i][0:rows, :], hf[0:rows, 0, t, HALVES[i % 2]],
                                  ALU.subtract).then_inc(S("hf_rest_ready"), 1)
                dve.wait_ge(S("hf_1_ready"), i + 1)
                dve.tensor_tensor(hf[0:rows, 2, t, HALVES[i % 2]], rest[0:rows, i % 2, :],
                                  hf[0:rows, 1, t, HALVES[i % 2]], ALU.subtract).then_inc(S("hf_2_ready"), 1)
            link(dve.memset(logit[:, :, :], 0.0))
            dve.wait_ge(S("logits_psum"), 1)
            dve.tensor_copy(logit[:, 0:2, :], B[6][:, 0:16].rearrange("p (t e) -> p t e", t=2))
            link(dve.tensor_copy(logit[0:16, 2, :], B[6][0:16, 16:24]))
            four = [P, NT, N_EXPERTS, N_EXPERTS]
            other = logit[:, :, :].unsqueeze(2).to_broadcast(four)
            self_ = logit[:, :, :].unsqueeze(3).to_broadcast(four)
            view = [c[:, :, :].rearrange("p t (e j) -> p t e j", e=N_EXPERTS) for c in (cmp_a, cmp_b)]
            dve.tensor_tensor(view[0], other, self_, ALU.is_gt)
            link(dve.tensor_tensor(view[1], other, self_, ALU.is_equal))
            tie = const[:, C_TIE:C_TIE + 64].unsqueeze(1).to_broadcast([P, NT, 64])
            link(dve.tensor_tensor(cmp_b[:, :, :], cmp_b[:, :, :], tie, ALU.mult))
            link(dve.tensor_tensor(cmp_a[:, :, :], cmp_a[:, :, :], cmp_b[:, :, :], ALU.add))
            link(dve.tensor_reduce(chosen[:, :, :], view[0], AX.X, ALU.add))
            dve.tensor_scalar(chosen[:, :, :], chosen[:, :, :], float(TOP_K), None, ALU.is_lt)\
                .then_inc(S("chosen_ready"), 1)
            link(dve.tensor_reduce(r_small[:, 0, :], logit[:, :, :], AX.X, ALU.max))
            three_e = [P, NT, N_EXPERTS]
            dve.tensor_tensor(r_exp[:, :, :], logit[:, :, :], r_small[:, 0, :].unsqueeze(2).to_broadcast(three_e),
                              ALU.subtract).then_inc(S("r_shifted"), 1)
            dve.wait_ge(S("r_exp_ready"), 1)
            dve.wait_ge(S("chosen_ready"), 1)
            link(dve.tensor_tensor(gate[:, :, :], r_exp[:, :, :], chosen[:, :, :], ALU.mult))
            link(dve.tensor_reduce(r_small[:, 1, :], gate[:, :, :], AX.X, ALU.add))
            link(dve.reciprocal(r_small[:, 2, :], r_small[:, 1, :]))
            link(dve.tensor_tensor(gate[:, :, :], gate[:, :, :],
                                   r_small[:, 2, :].unsqueeze(2).to_broadcast(three_e), ALU.mult))
            link(dve.memset(place[:, :, :], -1.0))
            link(dve.memset(place_1[:, :, :], 0.0))
            dve.wait_ge(S("ranks_psum"), 1)
            for t, (_, rows) in enumerate(TOKEN_TILES):
                last = dve.scalar_tensor_tensor(place_1[0:rows, t, :], B[5][0:rows, 8 * t:8 * t + 8], 1.0,
                                                chosen[0:rows, t, :], ALU.add, ALU.mult)
            link(last)
            for n in range(PASSES):
                last = dve.tensor_scalar(place[:, :, 8 * n:8 * n + 8], place_1[:, :, :], -1.0 - P * n, None, ALU.add)
            link(last)
            link(dve.tensor_reduce(r_small[0:1, 3, 0:1], B[5][0:1, 32:40], AX.X, ALU.max))
            dve.tensor_copy(count_i[0:1, 0:1], r_small[0:1, 3, 0:1]).then_inc(S("count_ready"), 1)
            for n in range(3):
                src = gate if n == 0 else gate_rest
                link(dve.tensor_copy(gate_part[:, n, :, :], src[:, :, :]))
                if n < 2:
                    link(dve.tensor_tensor(gate_rest[:, :, :], src[:, :, :], gate_part[:, n, :, :], ALU.subtract))
            pick_run(dve, 0)
            xe_lo_copy(dve, 0)
            for u in range(SPLIT):
                moe_lo(dve, 0, u)
            with dve.Fori(0, N_EXPERTS - 1) as m:
                run_vector(dve, m, m, False, True)
            run_vector(dve, N_EXPERTS - 1, N_EXPERTS - 1, False, False)
            overflow(dve, lambda m, e: run_vector(dve, m, e, True, False))
            link(dve.memset(ss[:, 0, :], 1.0))
            dve.drain().then_inc(S("acc_done"), 1)
            dve.wait_ge(S("last_std"), 1)
            link(dve.reciprocal(ss[:, 2, :], ss[:, 1, :]))
            dve.wait_ge(S("g_final_landed"), 16)
            for t, (_, rows) in enumerate(TOKEN_TILES):
                dve.scalar_tensor_tensor(y_out[0:rows, t, :], acc[0:rows, t, :], ss[0:rows, 2, t:t + 1],
                                         g_final[0:rows, :], ALU.mult, ALU.mult).then_inc(S("y_out_ready"), 1)

        @block.tensor
        def _(pe):
            pe.sem_inc(S("m_used"), SPLIT)
            pe.wait_ge(S("const_landed"), 16)
            pe.wait_ge(S("x_landed"), 64)
            for k in range(KD):
                for t, (t0, rows) in enumerate(TOKEN_TILES):
                    last = pe.transpose(B[k][:, t0:t0 + rows], x_rows[0:rows, t, k * P:(k + 1) * P],
                                        ident[0:rows, 0:rows])
                last.then_inc(S("x_transposed"), 1)
            pe.wait_ge(S("params_landed"), 160)
            pe.wait_ge(S("h0_ready"), 2)
            pe.transpose(B[1][:, 384:384 + N_PARAMS], p_rows[0:N_PARAMS, :],
                         ident[0:N_PARAMS, 0:N_PARAMS]).then_inc(S("params_transposed"), 1)
            pe.wait_ge(S("pool_set"), 1)
            for k in range(KD):
                norm_sum(pe, "n0", k, KD, B[0])

            def two_blocks(u, slot, banks2, block_ready=lambda k: None):
                pe.wait_ge(S("w_lo_ready"), u + 1)
                two_products(pe, slot, banks2, a_hi, a_lo, block_ready).then_inc(S("w_used"), 1)

            for u in range(U_X, U_G):
                if U_X + 2 <= u < U_Y + 2:
                    pe.wait_ge(S("x_evacuated"), u - 1)
                if u >= U_Y + 2:
                    pe.wait_ge(S("y_gate_ready"), u - U_Y - 1)
                two_blocks(u, u % 2, B[2 * (u % 2):2 * (u % 2) + 2],
                           lambda k: pe.wait_ge(S("n0_lo"), k + 1) if u == U_X else None)
            pe.wait_ge(S("y_gate_ready"), 4)
            pe.wait_ge(S("w_lo_ready"), U_G + 1)
            wh, wl = blocks_of(U_G % 2, 2048, 16)
            for k in range(N_BLOCKS):
                pe.wait_ge(S("xc_lo_ready"), k + 1)
                for g in range(2):
                    if k >= 4:
                        pe.wait_ge(S("gates_done"), 2 * (k - 4) + g + 1)
                    n = g * N_BLOCKS + k
                    last = three(pe, B[(2 * k + g) % 8][:, 0:T], wh[:, n, :], wl[:, n, :], b_hi[:, k, :],
                                 b_lo[:, k, :], True, True)
                    last.then_inc(S("gate_psum"), 1)
            pe.wait_ge(S("gate_psum"), 2 * N_BLOCKS)
            pe.sem_inc(S("w_used"), 1)
            pe.wait_ge(S("gates_done"), 2 * N_BLOCKS)
            pe.wait_ge(S("mixed_lo"), KD)
            residual_tensor(pe, "n1", "o_added", U_O, 4, 1, lambda q: dict(n=2048, k=8, xh=a_hi, xl=a_lo))
            with pe.Fori(0, KF // 2) as i:
                pe.wait_ge(S("silu_ready"), i + 1)
                two_blocks(U_F + 2 * i, U_F % 2, B[0:2], lambda k: pe.wait_ge(S("n1_lo"), k + 1))
                pe.wait_ge(S("g_ready"), 2 * i + 2)
                two_blocks(U_F + 1 + 2 * i, (U_F + 1) % 2, B[2:4])
            pe.wait_ge(S("g_lo_ready"), KF // 2 + 1)
            residual_tensor(pe, "n2", "w2_added", U_W2, 8, 2,
                            lambda q: dict(n=11 * 256, k=11, xh=g_hi, xl=g_lo, x0=11 * (q % 2),
                                           first=q % 2 == 0, last=q % 2 == 1))
            pe.wait_ge(S("w_lo_ready"), U_KV + 1)
            wh, wl = blocks_of(U_KV % 2, 8 * 320, KD)
            for k in range(KD):
                pe.wait_ge(S("n2_lo"), k + 1)
                for n, col in enumerate((0, P, 192)):
                    last = three(pe, B[n][:, 0:T], wh[:, k, col:col + P], wl[:, k, col:col + P], a_hi[:, k, :],
                                 a_lo[:, k, :], k == 0, k == KD - 1)
            last.then_inc(S("w_used"), 1)
            pe.wait_ge(S("n2b_lo"), KD)
            pe.wait_ge(S("w_lo_ready"), U_Q + 1)
            for n in range(KQ):
                last = product(pe, U_Q % 2, 3072, 8, P * n, B[3 + n], b_hi, b_lo)
                if n == 1:
                    for k in range(KC):
                        norm_sum(pe, "nk", k, KC, B[7])
            last.then_inc(S("w_used"), 1)
            for k in range(KQ):
                norm_sum(pe, "nq", k, KQ, B[6])
            pe.wait_ge(S("nk_lo"), KC)
            for s in range(HEADS + 3):
                if s < HEADS:
                    g, hh = s // 4, s % 4
                    slot = (U_H + g) % 2
                    kh, kl = (w[:, slot, 0:1024].rearrange("p (k n) -> p k n", k=KC) for w in (w_hi, w_lo))
                    qh, ql = (w[:, slot, 1024:1024 + 12 * P].rearrange("p (k n) -> p k n", k=KQ)
                              for w in (w_hi, w_lo))
                    if s:
                        pe.wait_ge(S("kq_ready"), s)
                        pe.wait_ge(S("q_ready"), s)
                    if hh == 0:
                        pe.wait_ge(S("w_lo_ready"), U_H + g + 1)
                        vh, vl = (w.rearrange("p k (h n) -> p k h n", h=4)[:, :, :, NOPE:NOPE + VH] for w in (kh, kl))
                        for t, (t0, rows) in enumerate(TOKEN_TILES):
                            o = (B[4][0:rows, 0:256], B[4][0:rows, 256:512], B[5][0:rows, 0:256])[t]
                            o = o.rearrange("p (h n) -> p h n", h=4)
                            for k in range(KC):
                                last = moving(pe, o, c_hi[:, k, t0:t0 + rows], c_lo[:, k, t0:t0 + rows],
                                              vh[:, k], vl[:, k], k == 0, k == KC - 1)
                        last.then_inc(S("v_psum"), 1)
                        pe.wait_ge(S("v_ready"), g + 1)
                    for k in range(KC):
                        c0 = hh * (NOPE + VH)
                        last = three(pe, B[4][0:NOPE, 0:T], kh[:, k, c0:c0 + NOPE], kl[:, k, c0:c0 + NOPE],
                                     c_hi[:, k, :], c_lo[:, k, :], k == 0, k == KC - 1)
                    last.then_inc(S("kq_psum"), 1)
                    if s == 0:
                        pe.wait_ge(S("nq_lo"), KQ)
                    for k in range(KQ):
                        c0 = hh * P
                        last = three(pe, B[5][:, 0:T], qh[:, k, c0:c0 + P], ql[:, k, c0:c0 + P], cq_hi[:, k, :],
                                     cq_lo[:, k, :], k == 0, k == KQ - 1)
                    last.then_inc(S("kq_psum"), 1)
                    if hh == 3:
                        pe.wait_ge(S("kq_psum"), 2 * s + 2)
                        pe.sem_inc(S("w_used"), 1)
                if s >= 3:
                    j, b = s - 3, (s - 3) % 2
                    pe.wait_ge(S("probT_ready"), j + 1)
                    if j >= 2 and j % 2 == 0:
                        pe.wait_ge(S("o_lo_ready"), j // 2)
                    g, c0, o0 = (j // 4) % 2, (j % 4) * VH, (j % 2) * VH
                    o = B[7][o0:o0 + VH, 0:T]
                    pe.matmul(o, v_sb[:, g, 0, c0:c0 + VH], probT[:, b, 0:T], start=True, stop=False)
                    pe.matmul(o[:, 64:T], v_sb[:, g, 1, c0:c0 + VH], probT[:, b, T:T + 208], start=False, stop=False)
                    pe.matmul(o[:, 192:T], v_sb[0:16, g, 2, c0:c0 + VH], probT2[0:16, b, :], start=False,
                              stop=True).then_inc(S("weighted"), 1)
                if 1 <= s <= HEADS:
                    j, b = s - 1, (s - 1) % 2
                    if j == 0:
                        pe.wait_ge(S("mask_rows"), 1)
                    pe.wait_ge(S("kq_ready"), j + 1)
                    pe.wait_ge(S("q_ready"), j + 1)
                    if j >= 2:
                        pe.wait_ge(S("exp_done"), j - 1)
                    n = QH + N_CHUNKS
                    for t, (t0, rows) in enumerate(TOKEN_TILES):
                        o = scores(b, t)
                        last = pe.matmul(o, q_head[0:n, b, t0:t0 + rows], k_head[0:n, b, 0:o.shape[1]],
                                         start=True, stop=True)
                    last.then_inc(S("scored"), 1)
                if 2 <= s < HEADS + 2:
                    j, b = s - 2, s % 2
                    pe.wait_ge(S("prob_ready"), j + 1)
                    pe.wait_ge(S("prob1_ready"), j + 1)
                    if j >= 2 and j % 2 == 0:
                        pe.wait_ge(S("o_lo_ready"), j // 2)
                    TP, OP = B[6], B[7]
                    pe.transpose(TP[:, 0:P], prob0[:, b, 0:P], ident)
                    pe.transpose(TP[:, P:2 * P], prob1[:, b, 0:P], ident)
                    pe.transpose(TP[:, 2 * P:T], prob2[0:16, b, 0:P], ident[0:16, 0:16])
                    pe.transpose(TP[:, T:T + 64], prob0[64:P, b, P:2 * P], ident[64:P, 64:P])
                    pe.transpose(TP[:, T + 64:T + 192], prob1[:, b, P:2 * P], ident)
                    pe.transpose(TP[:, T + 192:T + 208], prob2[0:16, b, P:2 * P], ident[0:16, 0:16])
                    pe.transpose(OP[0:16, T:T + 64], prob1[64:P, b, 2 * P:T], ident[64:P, 64:P])
                    pe.transpose(OP[0:16, T + 64:T + 80], prob2[0:16, b, 2 * P:T],
                                 ident[0:16, 0:16]).then_inc(S("p_transposed"), 1)
            pe.wait_ge(S("o_lo_ready"), KD)
            residual_tensor(pe, "n3", "ao_added", U_AO, 4, 1, lambda q: dict(n=2048, k=8, xh=a_hi, xl=a_lo))
            for name, src in (("h_rows", h), ("hf_rows", normed)):
                for i in range(2 * NT):
                    t0, rows = TOKEN_TILES[i // 2]
                    if src is normed:
                        pe.wait_ge(S("acc_set"), i + 1)
                        pe.wait_ge(S("n3_scaled"), 4 + 4 * (i % 2))
                    for kk in range(4):
                        k = 4 * (i % 2) + kk
                        last = pe.transpose(B[i][0:rows, kk * P:(kk + 1) * P], src[:, k, t0:t0 + rows], ident)
                    last.then_inc(S(name), 1)
            pe.wait_ge(S("router_landed"), 16)
            pe.wait_ge(S("n3_scaled"), KD)
            for t, (t0, rows) in enumerate(TOKEN_TILES):
                for k in range(KD):
                    last = pe.matmul(B[6][0:rows, 8 * t:8 * t + 8], normed[:, k, t0:t0 + rows], router[:, k, :],
                                     start=k == 0, stop=k == KD - 1)
            last.then_inc(S("logits_psum"), 1)
            pe.wait_ge(S("chosen_ready"), 1)
            pe.wait_ge(S("hf_2_ready"), 2 * NT)
            pe.wait_ge(S("ident_b_ready"), 1)
            tri = const[:, C_TRI:C_TRI + P]
            for t, (_, rows) in enumerate(TOKEN_TILES):
                for tt in range(t + 1):
                    r = TOKEN_TILES[tt][1]
                    pe.matmul(B[5][0:rows, 8 * t:8 * t + 8], (tri if tt == t else ones)[0:r, 0:rows],
                              chosen[0:r, tt, :], start=tt == 0, stop=tt == t)
            for tt, (_, r) in enumerate(TOKEN_TILES):
                last = pe.matmul(B[5][:, 32:40], ones[0:r, :], chosen[0:r, tt, :], start=tt == 0, stop=tt == NT - 1)
            last.then_inc(S("ranks_psum"), 1)
            pe.wait_ge(S("pick_ready"), 1)
            gather(pe, 0)
            with pe.Fori(0, N_EXPERTS) as m:
                run_tensor(pe, m)
            overflow(pe, lambda m, e: run_tensor(pe, m))


_INS = ["x", "meta_tokens", "norm_mix", "norm_ffn", "norm_final", "rnn_w_in", "rnn_conv_w", "rnn_conv_b",
        "rnn_w_a", "rnn_b_a", "rnn_w_i", "rnn_b_i", "rnn_lambda", "rnn_w_out", "kv_norm_src", "kv_w_down",
        "kv_latent_norm", "kv_w_up", "q_w_down", "q_latent_norm", "q_w_up", "attn_w_out", "ffn_w1", "ffn_w3",
        "ffn_w2", "moe_router", "moe_w1", "moe_w3", "moe_w2"]


def kernel(**inputs):
    import concourse.bacc as bacc
    from concourse.bass_utils import run_bass_kernel_spmd

    nc = bacc.Bacc("TRN2", target_bir_lowering=False, num_devices=1)
    arrays, args = {}, []
    for name in _INS:
        a = np.ascontiguousarray(inputs[name])
        arrays[f"in_{name}"] = a
        args.append(nc.dram_tensor(f"in_{name}", a.shape, mybir.dt.from_np(a.dtype), kind="ExternalInput").ap())
    arrays["consts"] = shape_constants()
    args.append(nc.dram_tensor("consts", (P, N_CONST), F32, kind="ExternalInput").ap())
    args.append(nc.dram_tensor("out", (1, SEQ, D), F32, kind="ExternalOutput").ap())
    trunk(nc, *args)
    r = run_bass_kernel_spmd(nc, [arrays], core_ids=[0])
    return r.results[0]["out"]
```

```python
from contextlib import ExitStack

import numpy as np

import concourse.bass as bass
from concourse import mybir

F32 = mybir.dt.float32
F32R = mybir.dt.float32r
BF16 = mybir.dt.bfloat16
I32 = mybir.dt.int32
ACT = mybir.ActivationFunctionType
ALU = mybir.AluOpType
AX = mybir.AxisListType

P = 128
D = 1024
KD = D // P
N_META = 16
SEQ = 256
T = N_META + SEQ
CHUNK = 64
TOKEN_TILES = [(0, 128), (128, 128), (256, 16)]
NT = len(TOKEN_TILES)
EPS = 1e-6
CONV = 4
N_BLOCKS = 8
LRU_C = 8.0
HEADS = 16
NOPE, ROPE, VH = 64, 32, 64
QH = NOPE + ROPE
Q_LORA, KV_LORA = 384, 256
KQ, KC = Q_LORA // P, KV_LORA // P
SCALE = float(1.0 / np.sqrt(QH))
MASK = -1e30
D_FF = 2816
KF = D_FF // P
N_EXPERTS = 8
TOP_K = 2
D_FFE = 3584

KEYS_OF_FIRST = 144

C_IDENT, C_TRI, C_IOTA, C_TIE = 0, 128, 256, 384
C_ROPE = 448
C_QMASK = C_ROPE + T
C_KMASK = C_QMASK + T
N_CONST = C_KMASK + T
N_CHUNKS = 1 + SEQ // CHUNK

PARAMS = [("norm_mix", 16), ("norm_ffn", 16), ("kv_src", 8), ("conv_w", 32), ("conv_b", 8),
          ("b_a", 8), ("b_i", 8), ("lam", 8), ("q_lat", 3), ("kv_lat", 2)]
PCOL = {}
_at = 0
for _name, _n in PARAMS:
    PCOL[_name] = _at
    _at += _n
N_PARAMS = _at

STEP = 512
STEPS = D_FFE // STEP
UNIT = 2048
RAW = 7
SPLIT = 3
UNITS = 6 * STEPS
PASSES = -(-T // P)
RUNS = N_EXPERTS * PASSES


def shape_constants():
    c = np.zeros((P, N_CONST), np.float32)
    i = np.arange(P)
    c[:, C_IDENT:C_IDENT + P] = np.eye(P)
    c[:, C_TRI:C_TRI + P] = i[:, None] < i[None, :]
    c[:, C_IOTA:C_IOTA + P] = i[None, :]
    e = np.arange(N_EXPERTS)
    c[:, C_TIE:C_TIE + 64] = (e[None, :] < e[:, None]).reshape(1, 64)
    half = ROPE // 2
    inv = (np.float32(10000.0) ** (-np.arange(0, ROPE, 2, dtype=np.float32) / np.float32(ROPE))).astype(np.float32)
    ang = (inv[:, None] * np.arange(T, dtype=np.float32)[None, :]).astype(np.float32)
    for o in (0, half):
        c[64 + o:64 + o + half, C_ROPE:C_ROPE + T] = np.cos(ang)
    c[96:96 + half, C_ROPE:C_ROPE + T] = -np.sin(ang)
    c[96 + half:96 + ROPE, C_ROPE:C_ROPE + T] = np.sin(ang)
    pos = np.arange(T)
    cid = np.where(pos < N_META, 0, 1 + (pos - N_META) // CHUNK)
    for n in range(N_CHUNKS):
        c[QH + n, C_QMASK:C_QMASK + T] = cid < n
        c[QH + n, C_KMASK:C_KMASK + T] = np.where(cid == n, MASK, 0.0)
    return c


class Units:

    def __init__(self):
        self.landed = [0, 0]
        self.arrived = []

    def add(self, n, dmas=1):
        first = len(self.arrived)
        for u in range(first, first + n):
            self.landed[u % 2] += 16 * dmas
            self.arrived.append(self.landed[u % 2])
        return first


def trunk(nc, x, meta_tokens, norm_mix, norm_ffn, norm_final, rnn_w_in, rnn_conv_w, rnn_conv_b,
          rnn_w_a, rnn_b_a, rnn_w_i, rnn_b_i, rnn_lambda, rnn_w_out, kv_norm_src, kv_w_down,
          kv_latent_norm, kv_w_up, q_w_down, q_latent_norm, q_w_up, attn_w_out, ffn_w1, ffn_w3,
          ffn_w2, moe_router, moe_w1, moe_w3, moe_w2, consts, out):
    ctx = ExitStack()
    with ctx:
        class Region:

            def __init__(self, at):
                self.at = at

            def sb(self, name, shape, dt=F32):
                n = (2 if dt == BF16 else 4) * int(np.prod(shape[1:]))
                t = nc.alloc_sbuf_tensor_at(name, shape, dt, offset=self.at)
                self.at += -(-n // 32) * 32
                return t

        base = -(-nc.sbuf_base // 64) * 64
        end = nc.sbuf_usable_end
        ctx.enter_context(nc.sbuf_tensor("slab", [P, (end - base) // 4 - 16], F32))

        fixed = Region(base)
        const = fixed.sb("const", [P, N_CONST])
        params = fixed.sb("params", [P, N_PARAMS])
        ones = fixed.sb("ones", [P, P])
        small = fixed.sb("small", [P, 2])
        eps = small[:, 0:1]
        count_i = fixed.sb("count_i", [P, 8], I32)
        router = fixed.sb("router", [P, KD, N_EXPERTS])
        sp_t = fixed.sb("sp_t", [P, 8, N_BLOCKS])
        split_at = fixed.at
        w_hi = fixed.sb("w_hi", [P, 2, 3072], F32R)
        w_lo = fixed.sb("w_lo", [P, 2, 3072], F32R)
        mixture_split = Region(split_at)
        m_hi = mixture_split.sb("m_hi", [P, SPLIT, UNIT], F32R)
        m_lo = mixture_split.sb("m_lo", [P, SPLIT, UNIT], F32R)
        raw_at = fixed.at
        m_raw = fixed.sb("m_raw", [P, RAW, UNIT])
        work_at = fixed.at

        rnn = Region(raw_at)
        x_pad = rnn.sb("x_pad", [P, KD, T + CONV - 1])
        x_conv = rnn.sb("x_conv", [P, KD, T])
        gate_r = rnn.sb("gate_r", [P, KD, T])
        gate_i = rnn.sb("gate_i", [P, KD, T])
        decay = rnn.sb("decay", [P, KD, T])
        tanh_z = rnn.sb("tanh_z", [P, KD, T])
        assert rnn.at <= work_at
        start = Region(raw_at + 2 * 8832)
        x_rows = start.sb("x_rows", [P, NT, D])
        p_rows = start.sb("p_rows", [P, P])
        ffn = Region(raw_at)
        g_hi = ffn.sb("g_hi", [P, KF, T], F32R)
        g_lo = ffn.sb("g_lo", [P, KF, T], F32R)
        silu = ffn.sb("silu", [P, 2, T])
        g_f32 = ffn.sb("g_f32", [P, 2, T])
        assert ffn.at <= work_at
        slot6 = Region(raw_at + (RAW - 1) * 4 * UNIT)
        latent_kv = slot6.sb("latent_kv", [P, KC, T])
        latent_q = slot6.sb("latent_q", [P, KQ, T])
        rope_a = slot6.sb("rope_a", [P, T])
        rope_b = slot6.sb("rope_b", [P, T])
        assert slot6.at <= work_at

        dense = Region(work_at)
        h = dense.sb("h", [P, KD, T])
        normed = dense.sb("normed", [P, KD, T])
        transition = dense.at
        raw = dense.sb("raw", [P, 2, 3072])
        std = dense.sb("std", [P, T])
        rstd = dense.sb("rstd", [P, T])
        sq = dense.sb("sq", [P, 4, T])
        a_at = dense.at
        a_hi = dense.sb("a_hi", [P, KD, T], F32R)
        a_lo = dense.sb("a_lo", [P, KD, T], F32R)
        b_at = dense.at
        b_hi = dense.sb("b_hi", [P, KD, T], F32R)
        b_lo = dense.sb("b_lo", [P, KD, T], F32R)
        y_gate = dense.sb("y_gate", [P, KD, T])
        assert dense.at <= end, (dense.at, end)
        att = Region(b_at + 2 * 4 * KD * T)
        c_hi = att.sb("c_hi", [P, KC, T], F32R)
        c_lo = att.sb("c_lo", [P, KC, T], F32R)
        cq_hi = att.sb("cq_hi", [P, KQ, T], F32R)
        cq_lo = att.sb("cq_lo", [P, KQ, T], F32R)
        k_head = att.sb("k_head", [P, 2, T])
        q_head = att.sb("q_head", [P, 2, T])
        n_max = att.sb("n_max", [P, 2, 4])
        bias_e = att.sb("bias_e", [P, 2, 4])
        p_sum = att.sb("p_sum", [P, 2, 4])
        p_inv = att.sb("p_inv", [P, 2, 4])
        assert att.at <= end, (att.at, end)
        probs_r = Region(b_at)
        v_sb = probs_r.sb("v_sb", [P, 2, NT, 4 * VH])
        prob0 = probs_r.sb("prob0", [P, 3, 256])
        probT = probs_r.sb("probT", [P, 2, T + 208])
        probT2 = probs_r.sb("probT2", [P, 2, 80])
        assert probs_r.at <= b_at + 2 * 4 * KD * T

        probs_n = Region(transition - 4 * KD * T)
        prob1 = probs_n.sb("prob1", [P, 3, T])
        prob2 = probs_n.sb("prob2", [P, 3, T])
        assert probs_n.at <= transition
        tokens_r = Region(transition)
        hf = tokens_r.sb("hf", [P, 3, NT, D], BF16)
        assert tokens_r.at <= a_at
        y_out = Region(transition).sb("y_out", [P, NT, D])
        moe = Region(a_at)
        acc = moe.sb("acc", [P, NT, D])
        g_final = moe.sb("g_final", [P, D])
        xe_hi = moe.sb("xe_hi", [P, KD, P], F32R)
        xe_lo = moe.sb("xe_lo", [P, KD, P], F32R)
        rest = Region(moe.at).sb("rest", [P, 2, STEP])
        silu_e = moe.sb("silu_e", [P, STEP])
        gated = moe.sb("gated", [P, STEP])
        gt_hi = moe.sb("gt_hi", [P, 2, 4, P], F32R)
        gt_lo = moe.sb("gt_lo", [P, 2, 4, P], F32R)
        routing = Region(moe.at)
        gate_rest = routing.sb("gate_rest", [P, NT, N_EXPERTS])
        logit = routing.sb("logit", [P, NT, N_EXPERTS])
        cmp_a = routing.sb("cmp_a", [P, NT, 64])
        cmp_b = routing.sb("cmp_b", [P, NT, 64])
        chosen = routing.sb("chosen", [P, NT, N_EXPERTS])
        gate = routing.sb("gate", [P, NT, N_EXPERTS])
        r_small = routing.sb("r_small", [P, 4, NT])
        r_exp = routing.sb("r_exp", [P, NT, N_EXPERTS])
        place_1 = routing.sb("place_1", [P, NT, N_EXPERTS])
        y_hi = moe.sb("y_hi", [P, D], F32R)
        y_lo = moe.sb("y_lo", [P, D], F32R)
        y_f32 = moe.sb("y_f32", [P, D])
        pick = moe.sb("pick", [P, NT, P], BF16)
        assert moe.at <= end, (moe.at, end)
        after = Region(base + 4 * C_ROPE)
        pickT = after.sb("pickT", [P, T], F32R)
        ident_b = after.sb("ident_b", [P, P], BF16)
        place = after.sb("place", [P, NT, RUNS + 2])
        gate_part = after.sb("gate_part", [P, 3, NT, N_EXPERTS], BF16)
        g_slot = after.sb("g_slot", [P, 1])
        ss = after.sb("ss", [P, 3, NT])
        assert after.at <= base + 4 * N_CONST

        banks = [ctx.enter_context(nc.psum_tensor(f"bank{i}", [P, 512], F32)) for i in range(8)]
        B = [b[:, :] for b in banks]

        names = {}

        def S(name):
            if name not in names:
                names[name] = ctx.enter_context(nc.semaphore(name))
            return names[name]

        def prm(name, k):
            c = PCOL[name] + k
            return params[:, c:c + 1]

        ident = const[:, C_IDENT:C_IDENT + P]

        units = Units()
        U_X = units.add(4)
        U_Y = units.add(1)
        U_G = units.add(1, 2)
        U_Y1 = units.add(3)
        U_O = units.add(4)
        U_F = units.add(2 * (KF // 2))
        U_W2 = units.add(8)
        U_KV = units.add(1)
        U_Q = units.add(1)
        U_H = units.add(4, 2)
        U_AO = units.add(4)
        n_units = len(units.arrived)

        def src_cols(w, c, n):
            return w.rearrange("(k p) n -> p k n", p=P)[:, :, bass.ds(c, n)]

        w_in_v = rnn_w_in.rearrange("o a b -> (o a) b")
        w_out_v = rnn_w_out.rearrange("o a b -> (o a) b")
        f1_v = ffn_w1.rearrange("o a b -> (o a) b")
        f3_v = ffn_w3.rearrange("o a b -> (o a) b")
        f2_v = ffn_w2.rearrange("o a b -> (o a) b")
        qd_v = q_w_down.rearrange("o a b -> (o a) b")
        qu_v = q_w_up.rearrange("o a b -> (o a) b")
        ao_v = attn_w_out.rearrange("o a b -> (o a) b")

        def raw_v(s, n, k):
            return raw[:, s, 0:n].rearrange("p (k n) -> p k n", k=k)

        def dma_unit(sp_, u, slot, pieces):
            if not isinstance(u, int) or u >= 2:
                sp_.wait_ge(S("w_lo_ready"), u - 1)
            for dst, src in pieces:
                sp_.dma_start(dst, src).then_inc(S(f"w_landed{slot}"), 16)

        def load_256(sp_, u, slot, w, c):
            dma_unit(sp_, u, slot, [(raw_v(slot, 2048, 8), src_cols(w, c, 256))])

        def parts(kind, slot):
            r, hi, lo = raw[:, slot, :], w_hi[:, slot, :], w_lo[:, slot, :]
            if isinstance(kind, int):
                cut = -(-(kind // 2) // 256) * 256
                return [[(r[:, a:b], hi[:, a:b], lo[:, a:b])] for a, b in ((0, cut), (cut, kind))]
            if kind == "kv_down":
                rv = r[:, 0:8 * 288].rearrange("p (k n) -> p k n", k=8)
                dst = [w[:, 0:8 * 320].rearrange("p (k n) -> p k n", k=8) for w in (hi, lo)]
                moves = [(0, 288, 0), (272, 288, 288), (256, 272, 304)]
                views = [(rv[:, :, a:b], *(d[:, :, c:c + b - a] for d in dst)) for a, b, c in moves]
                return [views[:1], views[1:]]
            rv = r[:, 1024:1024 + 12 * QH].rearrange("p (k n) -> p k n", k=12)
            dst = [w[:, 1024:1024 + 12 * P].rearrange("p (k n) -> p k n", k=12) for w in (hi, lo)]
            moves = [(0, QH, 0), (NOPE + 16, QH, QH), (NOPE, NOPE + 16, QH + 16)]
            views = [(rv[:, :, a:b], *(d[:, :, c:c + b - a] for d in dst)) for a, b, c in moves]
            return [[(r[:, 0:1024], hi[:, 0:1024], lo[:, 0:1024])], views]

        def split_hi(act, u, slot, kind, arrived, portions=(0, 1)):
            act.wait_ge(S(f"w_landed{slot}"), arrived)
            if not isinstance(u, int) or u >= 2:
                act.wait_ge(S("w_used"), u - 1)
            for portion in [parts(kind, slot)[n] for n in portions]:
                for r, hi, _ in portion:
                    last = act.activation(hi, r, ACT.Copy)
                last.then_inc(S("w_hi_ready"), 1)

        def split_lo(dve, u, slot, kind, portions=(0, 1)):
            for n in portions:
                dve.wait_ge(S("w_hi_ready"), 2 * u + n + 1)
                for r, hi, lo in parts(kind, slot)[n]:
                    last = dve.tensor_tensor(lo, r, hi.bitcast(F32), ALU.subtract)
            if 1 in portions:
                last.then_inc(S("w_lo_ready"), 1)

        KIND = {}
        for first, n, kind in ((U_X, 9, 2048), (U_O, 4, 2048), (U_F, KF, 2048), (U_W2, 8, 11 * 256),
                               (U_KV, 1, "kv_down"), (U_Q, 1, 3072), (U_H, 4, "heads"), (U_AO, 4, 2048)):
            for u in range(first, first + n):
                KIND[u] = kind

        def hi_of(act, u, portions=(0, 1)):
            if u < n_units:
                split_hi(act, u, u % 2, KIND[u], units.arrived[u], portions)

        def lo_of(dve, u, portions=(0, 1)):
            if u < n_units:
                split_lo(dve, u, u % 2, KIND[u], portions)

        def three(pe, o, wh, wl, xh, xl, first, last):
            pe.matmul(o, wh, xh, start=first, stop=False)
            pe.matmul(o, wh, xl, start=False, stop=False)
            return pe.matmul(o, wl, xh, start=False, stop=last)

        def blocks_of(slot, n, k):
            return [w[:, slot, 0:n].rearrange("p (k n) -> p k n", k=k) for w in (w_hi, w_lo)]

        def two_products(pe, slot, banks2, xh, xl, block_ready):
            wh, wl = blocks_of(slot, 2048, KD)
            for k in range(KD):
                block_ready(k)
                for j, bank in enumerate(banks2):
                    cols = slice(P * j, P * (j + 1))
                    ins = three(pe, bank[:, 0:T], wh[:, k, cols], wl[:, k, cols], xh[:, k, :], xl[:, k, :],
                                k == 0, k == KD - 1)
            return ins

        def product(pe, slot, n, k, col, bank, xh, xl, x0=0, first=True, last=True, m=P):
            wh, wl = blocks_of(slot, n, k)
            for kk in range(k):
                ins = three(pe, bank[0:m, 0:T], wh[:, kk, col:col + m], wl[:, kk, col:col + m],
                            xh[:, x0 + kk, :], xl[:, x0 + kk, :], first and kk == 0, last and kk == k - 1)
            return ins

        def norm_square(act, tag, k, src):
            if k >= 4:
                act.wait_ge(S(f"{tag}_summed"), k - 3)
            act.activation(sq[:, k % 4, :], src, ACT.Square).then_inc(S(f"{tag}_squared"), 1)

        def norm_sum(pe, tag, k, n, bank):
            pe.wait_ge(S(f"{tag}_squared"), k + 1)
            pe.matmul(bank[:, 0:T], ones[:, :], sq[:, k % 4, :], start=k == 0,
                      stop=k == n - 1).then_inc(S(f"{tag}_summed"), 1)

        def norm_table(act):
            act.activation(small[:, 1:2], eps, ACT.Sqrt)

        def norm_std(act, tag, n, bank):
            act.wait_ge(S(f"{tag}_summed"), n)
            act.activation(std[:, :], bank[:, 0:T], ACT.Sqrt, bias=eps,
                           scale=1.0 / (n * P)).then_inc(S(f"{tag}_std"), 1)

        def norm_inv(dve, tag):
            dve.wait_ge(S(f"{tag}_std"), 1)
            dve.reciprocal(rstd[:, :], std[:, :]).then_inc(S(f"{tag}_inv"), 1)
            dve.wait_ge(S(f"{tag}_inv"), 1)

        def norm_scale(dve, tag, n, src, gain, hi, lo):
            for k in range(n + 1):
                if k < n:
                    dve.scalar_tensor_tensor(normed[:, k, :], src[:, k, :], gain(k), rstd[:, :], ALU.mult,
                                             ALU.mult).then_inc(S(f"{tag}_scaled"), 1)
                if k:
                    dve.wait_ge(S(f"{tag}_hi"), k)
                    dve.tensor_tensor(lo[:, k - 1, :], normed[:, k - 1, :], hi[:, k - 1, :].bitcast(F32),
                                      ALU.subtract).then_inc(S(f"{tag}_lo"), 1)

        def norm_hi(act, tag, n, hi):
            for k in range(n):
                act.wait_ge(S(f"{tag}_scaled"), k + 1)
                act.activation(hi[:, k, :], normed[:, k, :], ACT.Copy).then_inc(S(f"{tag}_hi"), 1)

        def residual_scalar(act, tag, added, first, per):
            for q in range(4):
                for n in range(per):
                    hi_of(act, first + per * q + n + 2)
                if q == 0:
                    norm_table(act)
                for j in range(2):
                    k = 2 * q + j
                    act.wait_ge(S(added), k + 1)
                    norm_square(act, tag, k, h[:, k, :])

        def residual_vector(dve, added, first, per):
            for q in range(4):
                for n in range(per - 1):
                    lo_of(dve, first + per * q + 2 + n)
                dve.wait_ge(S("w_used"), first + per * (q + 1))
                for j in range(2):
                    k = 2 * q + j
                    dve.tensor_tensor(h[:, k, :], B[2 * (q % 2) + j][:, 0:T], h[:, k, :],
                                      ALU.add).then_inc(S(added), 1)
                lo_of(dve, first + per * q + per + 1)

        def residual_tensor(pe, tag, added, first, n_u, per, spec, block_ready=None):
            for q in range(n_u):
                u, grp = first + q, q // per
                if q % per == 0 and grp >= 2:
                    pe.wait_ge(S(added), 2 * (grp - 1))
                pe.wait_ge(S("w_lo_ready"), u + 1)
                s = dict(x0=0, first=True, last=True)
                s.update(spec(q))
                if q == 0 and block_ready:
                    last = two_products(pe, u % 2, B[0:2], s["xh"], s["xl"], block_ready)
                for j in range(0 if q == 0 and block_ready else 2):
                    last = product(pe, u % 2, s["n"], s["k"], P * j, B[2 * (grp % 2) + j], s["xh"], s["xl"],
                                   s["x0"], s["first"], s["last"])
                last.then_inc(S("w_used"), 1)
                if q % per == per - 1 and grp:
                    for k in (2 * grp - 2, 2 * grp - 1):
                        norm_sum(pe, tag, k, KD, B[7])
            for k in (KD - 2, KD - 1):
                norm_sum(pe, tag, k, KD, B[7])

        def scores(b, t):
            return (B[2 * b][:, 0:KEYS_OF_FIRST], B[2 * b + 1][:, 0:T], B[2 * b][0:16, 160:160 + T])[t]

        def rope(dve, bank, dsts, link):
            dve.tensor_tensor(rope_a[NOPE:QH, :], bank[NOPE:QH, 0:T], const[NOPE:QH, C_ROPE:C_ROPE + T], ALU.mult)
            link(dve.tensor_tensor(rope_b[NOPE:QH, :], bank[QH:P, 0:T], const[QH:P, C_ROPE:C_ROPE + T], ALU.mult))
            for dst in dsts:
                last = dve.tensor_tensor(dst, rope_a[NOPE:QH, :], rope_b[NOPE:QH, :], ALU.add)
            link(last)

        w1_v = moe_w1.rearrange("o e (k p) f -> (o e) p k f", p=P)
        w3_v = moe_w3.rearrange("o e (k p) f -> (o e) p k f", p=P)
        w2_v = moe_w2.rearrange("o e (j p) d -> (o e) p j d", p=P)

        ORDER = []
        for c in range(STEPS):
            ORDER += [("w1", c, 0), ("w1", c, 1), ("w3", c, 0), ("w3", c, 1)]
            if c:
                ORDER += [("w2", c - 1, 0), ("w2", c - 1, 1)]
        ORDER += [("w2", STEPS - 1, 0), ("w2", STEPS - 1, 1)]
        assert len(ORDER) == UNITS and UNITS % RAW == 0 and UNITS % SPLIT == 0
        LAST = STEPS - 1

        def moe_load(sp, expert, u):
            kind, c, half = ORDER[u]
            if kind == "w2":
                src = w2_v[bass.ds(expert, 1), :, 4 * c + 2 * half:4 * c + 2 * half + 2, :]
                dst = m_raw[:, u % RAW, :].rearrange("p (k n) -> p k n", k=2)
            else:
                v = w1_v if kind == "w1" else w3_v
                src = v[bass.ds(expert, 1), :, 4 * half:4 * half + 4, c * STEP:(c + 1) * STEP]
                dst = m_raw[:, u % RAW, :].rearrange("p (k n) -> p k n", k=4)
            sp.dma_start(dst, src.rearrange("a p k n -> (a p) k n")).then_inc(S(f"m_landed{u % RAW}"), 16)

        def moe_load_run(sp, m, expert, first=0):
            for u in range(first, UNITS):
                sp.wait_ge(S("m_lo_ready"), m * (2 * UNITS) + 2 * (u - RAW + 1))
                moe_load(sp, expert, u)

        HALF_UNITS = [slice(0, UNIT // 2), slice(UNIT // 2, UNIT)]

        def moe_hi(act, m, u):
            act.wait_ge(S(f"m_landed{u % RAW}"), m * (16 * (UNITS // RAW)) + 16 * (u // RAW + 1))
            act.wait_ge(S("m_used"), m * UNITS + (u + 1))
            for cols in HALF_UNITS:
                act.activation(m_hi[:, u % SPLIT, cols], m_raw[:, u % RAW, cols],
                               ACT.Copy).then_inc(S("m_hi_ready"), 1)

        def moe_lo(dve, m, u):
            for n, cols in enumerate(HALF_UNITS):
                dve.wait_ge(S("m_hi_ready"), m * (2 * UNITS) + (2 * u + n + 1))
                dve.tensor_tensor(m_lo[:, u % SPLIT, cols], m_raw[:, u % RAW, cols],
                                  m_hi[:, u % SPLIT, cols].bitcast(F32), ALU.subtract).then_inc(S("m_lo_ready"), 1)

        H1, H3, GT, Y0, Y1, G0, G1, SM = B
        HALVES = [slice(0, 512), slice(512, 1024)]
        SCATTER = [Y0, Y1, H3, GT]

        def used(m, u):
            return m * UNITS + (u + 1 + SPLIT)

        def gather(pe, m):
            for k in range(KD):
                for t, (_, rows) in enumerate(TOKEN_TILES):
                    for n in range(3):
                        last = pe.matmul((G0, G1)[k // 4][:, (k % 4) * P:(k % 4 + 1) * P],
                                         hf[0:rows, n, t, k * P:(k + 1) * P], pick[0:rows, t, :],
                                         start=t + n == 0, stop=t + n == NT + 1)
            last.then_inc(S("gathered"), 1)
            for t, (t0, rows) in enumerate(TOKEN_TILES):
                pe.transpose(SM.bitcast(BF16)[:, t0:t0 + rows], pick[0:rows, t, :], ident_b[0:rows, 0:rows])
            pe.wait_ge(S("gates_split"), 1)
            for t, (_, rows) in enumerate(TOKEN_TILES):
                for n in range(3):
                    last = pe.matmul(SM[:, 384:384 + N_EXPERTS], pick[0:rows, t, :],
                                     gate_part[0:rows, n, t, :], start=t + n == 0, stop=t + n == NT + 1)
            last.then_inc(S("pickT_done"), 1)

        def transpose_step(pe, m, c):
            pe.wait_ge(S("gated_ready"), m * STEPS + (c + 1))
            for j in range(4):
                last = pe.transpose(GT[:, j * P:(j + 1) * P], gated[:, j * P:(j + 1) * P], ident)
            last.then_inc(S("gt_done"), 1)

        def scatter(pe, m):
            for n in range(2):
                pe.wait_ge(S("y_ready"), 2 * m + (n + 1))
                for t, (t0, rows) in enumerate(TOKEN_TILES):
                    i = NT * n + t
                    if i >= len(SCATTER):
                        pe.wait_ge(S("acc_added"), 2 * NT * m + (i - len(SCATTER) + 2))
                    bank = SCATTER[i % len(SCATTER)]
                    pe.matmul(bank[0:rows, :], pickT[:, t0:t0 + rows], y_hi[:, HALVES[n]], start=True, stop=False)
                    pe.matmul(bank[0:rows, :], pickT[:, t0:t0 + rows], y_lo[:, HALVES[n]], start=False,
                              stop=True).then_inc(S("scattered"), 1)

        def gather_when_ready(pe, m):
            pe.wait_ge(S("pick_ready"), m + 1)
            pe.wait_ge(S("pickT_copied"), m)
            pe.wait_ge(S("gates_copied"), m)
            gather(pe, m)

        def run_tensor(pe, m, leading, following):
            if leading:
                gather_when_ready(pe, m)
            for u, (kind, c, half) in enumerate(ORDER):
                if u == 0:
                    pe.wait_ge(S("xe_ready"), m + 1)
                if kind == "w1" and half == 0:
                    pe.wait_ge(S("h1_free"), m * STEPS + (c + 1))
                if kind == "w3" and half == 0 and c:
                    transpose_step(pe, m, c - 1)
                if kind == "w3" and half == 0 and c == 0:
                    pe.wait_ge(S("acc_added"), 2 * NT * m + 1)
                if u == UNITS - 3:
                    transpose_step(pe, m, LAST)
                if kind == "w2" and half == 0:
                    pe.wait_ge(S("gt_ready"), m * STEPS + (c + 1))
                n = 2 if kind == "w2" else 4
                wh, wl = (w[:, u % SPLIT, :].rearrange("p (k n) -> p k n", k=n) for w in (m_hi, m_lo))
                for kk in range(n):
                    if kk % (n // 2) == 0:
                        pe.wait_ge(S("m_lo_ready"), m * (2 * UNITS) + (2 * u + kk // (n // 2) + 1))
                    k = n * half + kk
                    if kind == "w2":
                        for cols, bank in zip(HALVES, (Y0, Y1)):
                            last = moving(pe, bank, gt_hi[:, c % 2, k, :], gt_lo[:, c % 2, k, :], wh[:, kk, cols],
                                          wl[:, kk, cols], c == 0 and k == 0, c == LAST and k == 3)
                    else:
                        last = moving(pe, H1 if kind == "w1" else H3, xe_hi[:, k, :], xe_lo[:, k, :],
                                      wh[:, kk, :], wl[:, kk, :], k == 0, k == KD - 1)
                last.then_inc(S("m_used"), 1)
            if following:
                gather_when_ready(pe, m + 1)
            scatter(pe, m)

        def moving(pe, o, xh, xl, wh, wl, first, last):
            pe.matmul(o, xh, wh, start=first, stop=False)
            pe.matmul(o, xh, wl, start=False, stop=False)
            return pe.matmul(o, xl, wh, start=False, stop=last)

        def gt_hi_copy(act, m, c):
            act.wait_ge(S("gt_done"), m * STEPS + (c + 1))
            act.activation(gt_hi[:, c % 2, :, :], GT.rearrange("p (j n) -> p j n", j=4),
                           ACT.Copy).then_inc(S("gt_hi_ready"), 1)

        def xe_hi_copy(act, m):
            act.wait_ge(S("gathered"), m + 1)
            for i, bank in enumerate((G0, G1)):
                act.activation(xe_hi[:, 4 * i:4 * i + 4, :], bank.rearrange("p (j n) -> p j n", j=4),
                               ACT.Copy).then_inc(S("xe_hi_ready"), 1)

        def ahead(m, u, following):
            if u + SPLIT < UNITS:
                return m, u + SPLIT
            return (m + 1, u + SPLIT - UNITS) if following else None

        def run_scalar(act, m, leading, following):
            if leading:
                xe_hi_copy(act, m)
                for u in range(SPLIT):
                    moe_hi(act, m, u)
            for u, (kind, c, half) in enumerate(ORDER):
                nxt = ahead(m, u, following)
                if u == UNITS - 3:
                    gt_hi_copy(act, m, LAST)
                if nxt and u < UNITS - 1:
                    moe_hi(act, *nxt)
                if kind == "w1" and half == 1:
                    if c == 1:
                        act.wait_ge(S("pickT_done"), m + 1)
                        act.activation(pickT[:, :], SM.bitcast(BF16)[:, 0:T], ACT.Copy).then_inc(S("pickT_copied"), 1)
                    act.wait_ge(S("m_used"), used(m, u))
                    if c:
                        act.wait_ge(S("gated_ready"), m * STEPS + c)
                    act.activation(silu_e[:, :], H1, ACT.Silu).then_inc(S("h1_free"), 1)
                    if c:
                        gt_hi_copy(act, m, c - 1)
            for n in range(2):
                act.wait_ge(S("y_f32_ready"), 2 * m + (n + 1))
                act.activation(y_hi[:, HALVES[n]], y_f32[:, HALVES[n]], ACT.Copy).then_inc(S("y_hi_ready"), 1)
            if following:
                xe_hi_copy(act, m + 1)
                moe_hi(act, *ahead(m, UNITS - 1, True))

        def gt_lo_copy(dve, m, c):
            dve.wait_ge(S("gt_hi_ready"), m * STEPS + (c + 1))
            dve.tensor_tensor(gt_lo[:, c % 2, :, :], GT.rearrange("p (j n) -> p j n", j=4),
                              gt_hi[:, c % 2, :, :].bitcast(F32), ALU.subtract).then_inc(S("gt_ready"), 1)

        def xe_lo_copy(dve, m):
            for i, bank in enumerate((G0, G1)):
                dve.wait_ge(S("xe_hi_ready"), 2 * m + (i + 1))
                last = dve.tensor_tensor(xe_lo[:, 4 * i:4 * i + 4, :], bank.rearrange("p (j n) -> p j n", j=4),
                                         xe_hi[:, 4 * i:4 * i + 4, :].bitcast(F32), ALU.subtract)
            last.then_inc(S("xe_ready"), 1)

        def pick_run(dve, m):
            for t in range(NT):
                last = dve.tensor_scalar(pick[:, t, :], const[:, C_IOTA:C_IOTA + P],
                                         place[:, t, bass.ds(m, 1)], None, ALU.is_equal)
            last.then_inc(S("pick_ready"), 1)

        def run_vector(dve, m, expert, leading, following):
            if leading:
                xe_lo_copy(dve, m)
                for u in range(SPLIT):
                    moe_lo(dve, m, u)
            for u, (kind, c, half) in enumerate(ORDER):
                nxt = ahead(m, u, following)
                if kind == "w3" and half == 1:
                    dve.wait_ge(S("m_used"), used(m, u))
                    dve.wait_ge(S("h1_free"), m * STEPS + (c + 2))
                    if c:
                        dve.wait_ge(S("gt_hi_ready"), m * STEPS + c)
                    dve.tensor_tensor(gated[:, :], H3, silu_e[:, :], ALU.mult).then_inc(S("gated_ready"), 1)
                if u == UNITS - 3:
                    gt_lo_copy(dve, m, LAST)
                if nxt and u < UNITS - 1:
                    moe_lo(dve, *nxt)
                if kind == "w1" and half == 1 and c:
                    gt_lo_copy(dve, m, c - 1)
                    if c == 1:
                        dve.wait_ge(S("pickT_copied"), m + 1)
                        dve.tensor_copy(g_slot[:, 0:1], SM[:, bass.ds(expert + 384, 1)])\
                            .then_inc(S("gates_copied"), 1)
                        pick_run(dve, m + 1)
            dve.wait_ge(S("m_used"), used(m, UNITS - 1))
            dve.wait_ge(S("gates_copied"), m + 1)
            for n, bank in enumerate((Y0, Y1)):
                dve.tensor_scalar(y_f32[:, HALVES[n]], bank, g_slot[:, 0:1], None,
                                  ALU.mult).then_inc(S("y_f32_ready"), 1)
            for n in range(2):
                dve.wait_ge(S("y_hi_ready"), 2 * m + (n + 1))
                dve.tensor_tensor(y_lo[:, HALVES[n]], y_f32[:, HALVES[n]], y_hi[:, HALVES[n]].bitcast(F32),
                                  ALU.subtract).then_inc(S("y_ready"), 1)
            if following:
                xe_lo_copy(dve, m + 1)
            for n in range(2):
                for t, (_, rows) in enumerate(TOKEN_TILES):
                    i = NT * n + t
                    dve.wait_ge(S("scattered"), 2 * NT * m + (i + 1))
                    last = dve.tensor_tensor(acc[0:rows, t, HALVES[n]], SCATTER[i % len(SCATTER)][0:rows, :],
                                             acc[0:rows, t, HALVES[n]], ALU.add)
                    last.then_inc(S("acc_added"), 1)
            if following:
                moe_lo(dve, *ahead(m, UNITS - 1, True))

        def overflow(eng, body):
            eng.wait_ge(S("count_ready"), 1)
            most = eng.value_load(count_i[0:1, 0:1], min_val=0, max_val=T)
            with eng.If(most > P):
                with eng.Fori(1, PASSES) as again:
                    with eng.Fori(0, N_EXPERTS) as e:
                        body(again * N_EXPERTS + e, e)

        block = ctx.enter_context(nc.Block())

        @block.sync
        def _(sp):
            sp.dma_start(x_rows[0:N_META, 0, :], meta_tokens).then_inc(S("x_landed"), 16)
            sp.dma_start(x_rows[N_META:P, 0, :], x[0, 0:P - N_META, :]).then_inc(S("x_landed"), 16)
            sp.dma_start(x_rows[:, 1, :], x[0, P - N_META:2 * P - N_META, :]).then_inc(S("x_landed"), 16)
            sp.dma_start(x_rows[0:N_META, 2, :], x[0, 2 * P - N_META:SEQ, :]).then_inc(S("x_landed"), 16)
            for u in range(U_X, U_Y):
                load_256(sp, u, u % 2, w_in_v, D + 256 * u)
            load_256(sp, U_Y, U_Y % 2, w_in_v, 0)
            g_raw = raw[:, U_G % 2, 0:2048].rearrange("p (w n c) -> p w n c", w=2, n=N_BLOCKS)
            dma_unit(sp, U_G, U_G % 2, [(g_raw[:, 0], rnn_w_a.rearrange("o n c d -> (o c) n d")),
                                        (g_raw[:, 1], rnn_w_i.rearrange("o n c d -> (o c) n d"))])
            for q in range(3):
                load_256(sp, U_Y1 + q, (U_Y1 + q) % 2, w_in_v, 256 * (q + 1))
            for q in range(4):
                load_256(sp, U_O + q, (U_O + q) % 2, w_out_v, 256 * q)
            with sp.Fori(0, KF // 2) as i:
                load_256(sp, U_F + 2 * i, U_F % 2, f1_v, 256 * i)
                load_256(sp, U_F + 1 + 2 * i, (U_F + 1) % 2, f3_v, 256 * i)
            for q in range(8):
                u, half = U_W2 + q, q % 2
                rows = f2_v[half * (D_FF // 2):(half + 1) * (D_FF // 2), :]
                dma_unit(sp, u, u % 2, [(raw_v(u % 2, 11 * 256, 11), src_cols(rows, 256 * (q // 2), 256))])
            dma_unit(sp, U_KV, U_KV % 2, [(raw_v(U_KV % 2, 8 * 288, 8), src_cols(kv_w_down, 0, 288))])
            dma_unit(sp, U_Q, U_Q % 2, [(raw_v(U_Q % 2, 8 * Q_LORA, 8), src_cols(qd_v, 0, Q_LORA))])

            def load_heads(g):
                u = U_H + g
                dma_unit(sp, u, u % 2,
                         [(raw_v(u % 2, 1024, 2), src_cols(kv_w_up, 512 * g, 512)),
                          (raw[:, u % 2, 1024:1024 + 12 * QH].rearrange("p (k n) -> p k n", k=KQ),
                           src_cols(qu_v, 4 * QH * g, 4 * QH))])

            load_heads(0)
            load_heads(1)
            sp.wait_ge(S("w_used"), U_KV)
            for u in range(3):
                moe_load(sp, 0, u)
            load_heads(2)
            load_heads(3)
            for u in range(3, RAW - 1):
                moe_load(sp, 0, u)
            for q in range(4):
                load_256(sp, U_AO + q, (U_AO + q) % 2, ao_v, 256 * q)
                if q == 1:
                    sp.wait_ge(S("q_ready"), HEADS)
                    moe_load(sp, 0, RAW - 1)
            sp.wait_ge(S("w_used"), n_units)
            sp.dma_start(g_final[:, :], norm_final.partition_broadcast(P)).then_inc(S("g_final_landed"), 16)
            moe_load_run(sp, 0, 0, RAW)
            with sp.Fori(1, N_EXPERTS) as m:
                moe_load_run(sp, m, m)
            overflow(sp, lambda m, e: moe_load_run(sp, m, e))
            for t, (t0, rows) in enumerate(TOKEN_TILES):
                skip = N_META if t == 0 else 0
                sp.wait_ge(S("y_out_ready"), t + 1)
                sp.dma_start(out[0, t0 + skip - N_META:t0 + rows - N_META, :],
                             y_out[skip:rows, t, :]).then_inc(S("out_landed"), 16)
            sp.wait_ge(S("out_landed"), 16 * NT)

        @block.gpsimd
        def _(pool):
            pool.memset(ones[:, :], 1.0)
            pool.memset(eps, EPS)
            pool.memset(x_pad[:, :, 0:CONV - 1], 0.0).then_inc(S("pool_set"), 1)
            for k in range(KD):
                pool.wait_ge(S("xc_hi_ready"), k + 1)
                pool.tensor_tensor(b_lo[:, k, :], x_conv[:, k, :], b_hi[:, k, :].bitcast(F32),
                                   ALU.subtract).then_inc(S("xc_lo_ready"), 1)
            for k in range(N_BLOCKS):
                pool.wait_ge(S("gates_done"), 2 * k + 2)
                pool.tensor_tensor(gate_i[:, k, :], gate_i[:, k, :], x_conv[:, k, :],
                                   ALU.mult).then_inc(S("gated_x"), 1)
            pool.wait_ge(S("w_used"), U_H)
            pool.memset(prob0[:, :, :], 0.0).then_inc(S("prob0_cleared"), 1)
            for j in range(HEADS):
                pool.wait_ge(S("p_inv_ready"), j + 1)
                b = j % 2
                r = j % 3
                pool.tensor_scalar(prob0[:, r, 0:KEYS_OF_FIRST], prob0[:, r, 0:KEYS_OF_FIRST],
                                   p_inv[:, b, 0:1], None, ALU.mult)
                pool.tensor_scalar(prob2[0:16, r, :], prob2[0:16, r, :], p_inv[0:16, b, 2:3], None,
                                   ALU.mult).then_inc(S("prob_ready"), 1)

        @block.scalar
        def _(act):
            act.sem_inc(S("silu_ready"), 1)
            act.sem_inc(S("h1_free"), 1)
            act.dma_start(const[:, :], consts).then_inc(S("const_landed"), 16)
            row = 0
            for src in (norm_mix.rearrange("l (k p) -> (l k) p", p=P), norm_ffn.rearrange("l (k p) -> (l k) p", p=P),
                        kv_norm_src.rearrange("(k p) -> k p", p=P),
                        rnn_conv_w.rearrange("o w (k p) -> (o w k) p", p=P),
                        rnn_conv_b.rearrange("o (k p) -> (o k) p", p=P), rnn_b_a.rearrange("o (k p) -> (o k) p", p=P),
                        rnn_b_i.rearrange("o (k p) -> (o k) p", p=P), rnn_lambda.rearrange("o (k p) -> (o k) p", p=P),
                        q_latent_norm.rearrange("o (k p) -> (o k) p", p=P),
                        kv_latent_norm.rearrange("(k p) -> k p", p=P)):
                n = src.shape[0]
                act.dma_start(p_rows[row:row + n, :], src).then_inc(S("params_landed"), 16)
                row += n
            act.dma_start(router[:, :, :], moe_router.rearrange("o (k p) e -> (o p) k e", p=P))\
                .then_inc(S("router_landed"), 16)
            act.wait_ge(S("pool_set"), 1)
            for k in range(KD):
                if k == KD // 2:
                    hi_of(act, U_X)
                    hi_of(act, U_X + 1)
                act.wait_ge(S("h0_ready"), k + 1)
                norm_square(act, "n0", k, h[:, k, :])
            norm_table(act)
            norm_std(act, "n0", KD, B[0])
            norm_hi(act, "n0", KD, a_hi)
            act.wait_ge(S("neg_abs_ready"), 1)
            act.activation(sp_t[:, 1, :], sp_t[:, 0, :], ACT.Exp).then_inc(S("exp_lam"), 1)

            def conv_hi(u):
                for k in (2 * u, 2 * u + 1):
                    act.wait_ge(S("conv_ready"), k + 1)
                    act.activation(b_hi[:, k, :], x_conv[:, k, :], ACT.Copy).then_inc(S("xc_hi_ready"), 1)

            for u in range(4):
                hi_of(act, U_X + u + 2)
                if u:
                    conv_hi(u - 1)
            conv_hi(3)
            hi_of(act, U_Y1)
            for k in range(N_BLOCKS):
                for g, (bias, dst) in enumerate((("b_a", gate_r), ("b_i", gate_i))):
                    act.wait_ge(S("gate_psum"), 2 * k + g + 1)
                    act.activation(dst[:, k, :], B[4 + (2 * k + g) % 4][:, 0:T], ACT.Sigmoid,
                                   bias=prm(bias, k)).then_inc(S("gates_done"), 1)
            hi_of(act, U_Y1 + 1)
            for part in range(2):
                ks = slice(4 * part, 4 * part + 4)
                act.wait_ge(S("z_ready"), 4 * part + 4)
                act.activation(decay[:, ks, :], tanh_z[:, ks, :], ACT.Exp, scale=-1.0)
                act.activation(gate_r[:, ks, :], tanh_z[:, ks, :], ACT.Exp, scale=-2.0).then_inc(S("decays"), 1)
                act.wait_ge(S("decays"), part + 1)
                act.activation(tanh_z[:, ks, :], tanh_z[:, ks, :], ACT.Tanh).then_inc(S("tanh_ready"), 1)
            hi_of(act, U_Y1 + 2)
            for part in range(2):
                ks = slice(4 * part, 4 * part + 4)
                act.wait_ge(S("one_less_sq"), part + 1)
                act.activation(tanh_z[:, ks, :], gate_r[:, ks, :], ACT.Sqrt).then_inc(S("mult_ready"), 1)
            hi_of(act, U_O)
            for q in range(4):
                act.wait_ge(S("w_used"), U_Y + 1 if q == 0 else U_Y1 + q)
                for j in range(2):
                    last = act.activation(y_gate[:, 2 * q + j, :], B[2 * q + j][:, 0:T], ACT.Gelu_apprx_tanh)
                last.then_inc(S("y_gate_ready"), 1)
            for k in range(KD):
                act.wait_ge(S("mixed"), k + 1)
                act.activation(a_hi[:, k, :], gate_r[:, k, :], ACT.Copy).then_inc(S("mixed_hi"), 1)
            hi_of(act, U_O + 1)
            residual_scalar(act, "n1", "o_added", U_O, 1)
            norm_std(act, "n1", KD, B[7])
            norm_hi(act, "n1", KD, a_hi)

            def up_step(i):
                act.wait_ge(S("w_used"), U_F + 1 + 2 * i)
                for j in range(2):
                    last = act.activation(silu[:, j, :], B[j][:, 0:T], ACT.Silu)
                last.then_inc(S("silu_ready"), 1)

            def up_hi(i):
                for j in range(2):
                    act.wait_ge(S("g_ready"), 2 * i + (j + 3))
                    act.activation(g_hi[:, bass.ds(2 * i + j, 1), :], g_f32[:, j:j + 1, :],
                                   ACT.Copy).then_inc(S("g_hi_ready"), 1)

            with act.Fori(0, KF // 2 - 1) as i:
                up_step(i)
                split_hi(act, U_F + 2 + 2 * i, U_F % 2, 2048, units.arrived[U_F + 2] + 16 * i)
                split_hi(act, U_F + 3 + 2 * i, (U_F + 1) % 2, 2048, units.arrived[U_F + 3] + 16 * i)
                up_hi(i)
            up_step(KF // 2 - 1)
            hi_of(act, U_W2)
            hi_of(act, U_W2 + 1)
            up_hi(KF // 2 - 1)
            residual_scalar(act, "n2", "w2_added", U_W2, 2)
            norm_std(act, "n2", KD, B[7])
            norm_hi(act, "n2", KD, a_hi)
            norm_hi(act, "n2b", KD, b_hi)
            norm_table(act)
            for k in range(KC):
                act.wait_ge(S("latent_kv_ready"), k + 1)
                norm_square(act, "nk", k, latent_kv[:, k, :])
            for b in range(2):
                act.activation(q_head[96:96 + N_CHUNKS, b, :], const[96:96 + N_CHUNKS, C_QMASK:C_QMASK + T], ACT.Copy)
                last = act.activation(k_head[96:96 + N_CHUNKS, b, :], const[96:96 + N_CHUNKS, C_KMASK:C_KMASK + T],
                                      ACT.Copy)
            last.then_inc(S("mask_rows"), 1)
            hi_of(act, U_H)
            act.wait_ge(S("nk_summed"), KC)
            norm_std(act, "nk", KC, B[7])
            norm_hi(act, "nk", KC, c_hi)
            for k in range(KQ):
                act.wait_ge(S("latent_q_ready"), k + 1)
                norm_square(act, "nq", k, latent_q[:, k, :])
            act.wait_ge(S("nk_inv"), 1)
            norm_std(act, "nq", KQ, B[6])
            norm_hi(act, "nq", KQ, cq_hi)
            for s in range(HEADS + 4):
                if s >= 4:
                    j, b = s - 4, s % 2
                    act.wait_ge(S("p_transposed"), j + 1)
                    if j >= 2:
                        act.wait_ge(S("weighted"), j - 1)
                    act.activation(probT[:, b, :], B[6][:, 0:T + 208], ACT.Copy)
                    act.activation(probT2[0:16, b, :], B[7][0:16, T:T + 80], ACT.Copy).then_inc(S("probT_ready"), 1)
                if 2 <= s < HEADS + 2:
                    j, b = s - 2, s % 2
                    act.wait_ge(S("bias_ready"), j + 1)
                    if j == 0:
                        act.wait_ge(S("prob0_cleared"), 1)
                    if j >= 3:
                        act.wait_ge(S("p_transposed"), j - 2)
                    r = j % 3
                    for t, (_, rows) in enumerate(TOKEN_TILES):
                        dst = (prob0[:, r, 0:KEYS_OF_FIRST], prob1[:, r, :], prob2[0:rows, r, :])[t]
                        last = act.activation(dst, scores(b, t), ACT.Exp, bias=bias_e[0:rows, b, t:t + 1],
                                              scale=SCALE, accum_out=p_sum[0:rows, b, t:t + 1])
                    last.then_inc(S("exp_done"), 1)
                if s < HEADS:
                    b = s % 2
                    if s >= 2:
                        act.wait_ge(S("scored"), s - 1)
                    act.wait_ge(S("kq_psum"), 2 * s + 1)
                    act.activation(k_head[0:NOPE, b, :], B[4][0:NOPE, 0:T], ACT.Copy)
                    act.wait_ge(S("kq_psum"), 2 * s + 2)
                    act.activation(q_head[0:NOPE, b, :], B[5][0:NOPE, 0:T], ACT.Copy).then_inc(S("kq_ready"), 1)
                if s >= 5 and s % 2:
                    k = (s - 5) // 2
                    act.wait_ge(S("weighted"), s - 3)
                    act.activation(a_hi[:, k, :], B[7][:, 0:T], ACT.Copy).then_inc(S("o_hi_ready"), 1)
                if s % 4 in (1, 2):
                    hi_of(act, U_H + s // 4 + 1, (s % 4 - 1,))
            residual_scalar(act, "n3", "ao_added", U_AO, 1)
            norm_std(act, "n3", KD, B[7])
            for i in range(2 * NT):
                t, rows = i // 2, TOKEN_TILES[i // 2][1]
                act.wait_ge(S("h_rows"), i + 1)
                act.activation(acc[0:rows, t, HALVES[i % 2]], B[i][0:rows, :], ACT.Copy).then_inc(S("acc_set"), 1)
            for i in range(2 * NT + 1):
                if i < 2 * NT:
                    t, rows = i // 2, TOKEN_TILES[i // 2][1]
                    act.wait_ge(S("hf_rows"), i + 1)
                    act.activation(hf[0:rows, 0, t, HALVES[i % 2]], B[i][0:rows, :], ACT.Copy)\
                        .then_inc(S("hf_0_ready"), 1)
                if i:
                    t, rows = (i - 1) // 2, TOKEN_TILES[(i - 1) // 2][1]
                    act.wait_ge(S("hf_rest_ready"), i)
                    act.activation(hf[0:rows, 1, t, HALVES[(i - 1) % 2]], rest[0:rows, (i - 1) % 2, :], ACT.Copy)\
                        .then_inc(S("hf_1_ready"), 1)
            act.activation(ident_b[:, :], ident, ACT.Copy).then_inc(S("ident_b_ready"), 1)
            act.wait_ge(S("r_shifted"), 1)
            act.activation(r_exp[:, :, :], r_exp[:, :, :], ACT.Exp).then_inc(S("r_exp_ready"), 1)
            act.wait_ge(S("w_used"), n_units)
            for u in range(SPLIT):
                moe_hi(act, 0, u)
            xe_hi_copy(act, 0)
            with act.Fori(0, N_EXPERTS - 1) as m:
                run_scalar(act, m, False, True)
            run_scalar(act, N_EXPERTS - 1, False, False)
            overflow(act, lambda m, e: run_scalar(act, m, True, False))
            act.wait_ge(S("acc_done"), 1)
            for t, (_, rows) in enumerate(TOKEN_TILES):
                last = act.activation(y_out[0:rows, t, :], acc[0:rows, t, :], ACT.Square,
                                      accum_out=ss[0:rows, 0, t:t + 1])
            last.then_inc(S("ss_ready"), 1)
            act.wait_ge(S("ss_ready"), 1)
            act.activation(ss[:, 1, :], ss[:, 0, :], ACT.Sqrt, bias=eps, scale=1.0 / D).then_inc(S("last_std"), 1)

        @block.vector
        def _(dve):
            own = [0]

            def link(ins):
                own[0] += 1
                ins.then_inc(S("dve_own"), 1)
                dve.wait_ge(S("dve_own"), own[0])

            dve.sem_inc(S("acc_added"), 1)
            dve.sem_inc(S("g_ready"), 2)
            dve.sem_inc(S("g_lo_ready"), 1)
            for k in range(KD):
                dve.wait_ge(S("x_transposed"), k + 1)
                dve.tensor_copy(h[:, k, :], B[k][:, 0:T]).then_inc(S("h0_ready"), 1)
            lo_of(dve, U_X)
            lo_of(dve, U_X + 1)
            dve.wait_ge(S("params_transposed"), 1)
            link(dve.tensor_copy(params[:, :], B[1][:, 384:384 + N_PARAMS]))
            norm_inv(dve, "n0")
            norm_scale(dve, "n0", KD, h, lambda k: prm("norm_mix", k), a_hi, a_lo)
            lam = params[:, PCOL["lam"]:PCOL["lam"] + N_BLOCKS]
            link(dve.tensor_scalar(sp_t[:, 2, :], lam, -1.0, None, ALU.mult))
            link(dve.tensor_tensor(sp_t[:, 0, :], sp_t[:, 2, :], lam, ALU.min))
            dve.sem_inc(S("neg_abs_ready"), 1)
            dve.tensor_scalar(sp_t[:, 2, :], sp_t[:, 2, :], 0.0, None, ALU.max)
            dve.wait_ge(S("exp_lam"), 1)
            link(dve.tensor_scalar(sp_t[:, 3, :], sp_t[:, 1, :], 2.0, None, ALU.add))
            link(dve.reciprocal(sp_t[:, 4, :], sp_t[:, 3, :]))
            link(dve.tensor_tensor(sp_t[:, 3, :], sp_t[:, 1, :], sp_t[:, 4, :], ALU.mult))
            link(dve.tensor_tensor(sp_t[:, 4, :], sp_t[:, 3, :], sp_t[:, 3, :], ALU.mult))
            link(dve.tensor_scalar(sp_t[:, 5, :], sp_t[:, 4, :], 1.0 / 17, None, ALU.mult))
            for n in range(7, 0, -1):
                link(dve.scalar_tensor_tensor(sp_t[:, 5, :], sp_t[:, 5, :], 1.0 / (2 * n + 1), sp_t[:, 4, :],
                                              ALU.add, ALU.mult))
            link(dve.scalar_tensor_tensor(sp_t[:, 5, :], sp_t[:, 5, :], 1.0, sp_t[:, 3, :], ALU.add, ALU.mult))
            link(dve.scalar_tensor_tensor(sp_t[:, 6, :], sp_t[:, 5, :], 2.0, sp_t[:, 2, :], ALU.mult, ALU.add))
            dve.tensor_scalar(sp_t[:, 7, :], sp_t[:, 6, :], LRU_C, None, ALU.mult).then_inc(S("z_gain_ready"), 1)
            dve.wait_ge(S("n0_lo"), KD)
            dve.wait_ge(S("pool_set"), 1)
            for u in range(4):
                dve.wait_ge(S("w_used"), U_X + u + 1)
                for j in range(2):
                    last = dve.tensor_copy(x_pad[:, 2 * u + j, CONV - 1:], B[2 * (u % 2) + j][:, 0:T])
                last.then_inc(S("x_evacuated"), 1)
                dve.wait_ge(S("x_evacuated"), u + 1)
                for w in range(CONV):
                    for k in (2 * u, 2 * u + 1):
                        tap = x_pad[:, k, w:w + T]
                        if w == 0:
                            last = dve.tensor_scalar(x_conv[:, k, :], tap, prm("conv_w", k), prm("conv_b", k),
                                                     ALU.mult, ALU.add)
                        else:
                            last = dve.scalar_tensor_tensor(x_conv[:, k, :], tap, prm("conv_w", 8 * w + k),
                                                            x_conv[:, k, :], ALU.mult, ALU.add)
                        if w == CONV - 1:
                            last.then_inc(S("conv_ready"), 1)
                    if w < CONV - 1:
                        link(last)
                    if w == 1:
                        lo_of(dve, U_X + u + 2)
            lo_of(dve, U_Y1)
            dve.wait_ge(S("z_gain_ready"), 1)
            for k in range(N_BLOCKS):
                dve.wait_ge(S("gates_done"), 2 * k + 1)
                dve.tensor_scalar(tanh_z[:, k, :], gate_r[:, k, :], sp_t[:, 7, k:k + 1], None,
                                  ALU.mult).then_inc(S("z_ready"), 1)
            lo_of(dve, U_Y1 + 1)
            for part in range(2):
                ks = slice(4 * part, 4 * part + 4)
                dve.wait_ge(S("tanh_ready"), part + 1)
                dve.scalar_tensor_tensor(gate_r[:, ks, :], gate_r[:, ks, :], 1.0, tanh_z[:, ks, :], ALU.add,
                                         ALU.mult).then_inc(S("one_less_sq"), 1)
            lo_of(dve, U_Y1 + 2)
            for part in range(2):
                ks = slice(4 * part, 4 * part + 4)
                dve.wait_ge(S("mult_ready"), part + 1)
                dve.wait_ge(S("gated_x"), 4 * part + 4)
                link(dve.tensor_tensor(gate_i[:, ks, :], tanh_z[:, ks, :], gate_i[:, ks, :], ALU.mult))
                for k in range(4 * part, 4 * part + 4):
                    last = dve.tensor_tensor_scan(x_conv[:, k, :], decay[:, k, :], gate_i[:, k, :], 0.0,
                                                  ALU.mult, ALU.add)
                link(last)
            lo_of(dve, U_O)
            dve.wait_ge(S("y_gate_ready"), 4)
            for k in range(KD + 1):
                if k < KD:
                    dve.tensor_tensor(gate_r[:, k, :], x_conv[:, k, :], y_gate[:, k, :],
                                      ALU.mult).then_inc(S("mixed"), 1)
                if k:
                    dve.wait_ge(S("mixed_hi"), k)
                    dve.tensor_tensor(a_lo[:, k - 1, :], gate_r[:, k - 1, :], a_hi[:, k - 1, :].bitcast(F32),
                                      ALU.subtract).then_inc(S("mixed_lo"), 1)
            lo_of(dve, U_O + 1)
            residual_vector(dve, "o_added", U_O, 1)
            norm_inv(dve, "n1")
            norm_scale(dve, "n1", KD, h, lambda k: prm("norm_ffn", k), a_hi, a_lo)

            def up_product(i):
                dve.wait_ge(S("w_used"), U_F + 2 + 2 * i)
                dve.wait_ge(S("silu_ready"), i + 2)
                dve.wait_ge(S("g_lo_ready"), i + 1)
                for j in range(2):
                    dve.tensor_tensor(g_f32[:, j, :], B[2 + j][:, 0:T], silu[:, j, :],
                                      ALU.mult).then_inc(S("g_ready"), 1)

            def up_lo(i):
                for j in range(2):
                    dve.wait_ge(S("g_hi_ready"), 2 * i + (j + 1))
                    last = dve.tensor_tensor(g_lo[:, bass.ds(2 * i + j, 1), :], g_f32[:, j:j + 1, :],
                                             g_hi[:, bass.ds(2 * i + j, 1), :].bitcast(F32), ALU.subtract)
                last.then_inc(S("g_lo_ready"), 1)

            with dve.Fori(0, KF // 2 - 1) as i:
                split_lo(dve, U_F + 2 + 2 * i, U_F % 2, 2048)
                up_product(i)
                split_lo(dve, U_F + 3 + 2 * i, (U_F + 1) % 2, 2048)
                up_lo(i)
            lo_of(dve, U_W2)
            up_product(KF // 2 - 1)
            lo_of(dve, U_W2 + 1)
            up_lo(KF // 2 - 1)
            residual_vector(dve, "w2_added", U_W2, 2)

            def evacuate_values(g):
                dve.wait_ge(S("v_psum"), g + 1)
                dve.tensor_copy(v_sb[:, g % 2, 0:2, :], B[4].rearrange("p (t n) -> p t n", t=2))
                dve.tensor_copy(v_sb[0:16, g % 2, 2, :], B[5][0:16, 0:256]).then_inc(S("v_ready"), 1)

            norm_inv(dve, "n2")
            norm_scale(dve, "n2", KD, h, lambda k: prm("kv_src", k), a_hi, a_lo)
            norm_scale(dve, "n2b", KD, h, lambda k: prm("norm_mix", KD + k), b_hi, b_lo)
            dve.wait_ge(S("w_used"), U_KV + 1)
            for k in range(KC):
                dve.tensor_copy(latent_kv[:, k, :], B[k][:, 0:T]).then_inc(S("latent_kv_ready"), 1)
            rope(dve, B[2], [k_head[NOPE:QH, 0, :], k_head[NOPE:QH, 1, :]], link)
            dve.memset(n_max[:, :, :], 0.0)
            link(dve.memset(p_sum[:, :, :], 1.0))
            lo_of(dve, U_H)
            norm_inv(dve, "nk")
            norm_scale(dve, "nk", KC, latent_kv, lambda k: prm("kv_lat", k), c_hi, c_lo)
            dve.wait_ge(S("w_used"), U_Q + 1)
            for k in range(KQ):
                dve.tensor_copy(latent_q[:, k, :], B[3 + k][:, 0:T]).then_inc(S("latent_q_ready"), 1)
            norm_inv(dve, "nq")
            evacuate_values(0)
            norm_scale(dve, "nq", KQ, latent_q, lambda k: prm("q_lat", k), cq_hi, cq_lo)
            for s in range(HEADS + 4):
                if s and s < HEADS and s % 4 == 0:
                    evacuate_values(s // 4)
                if 2 <= s < HEADS + 2:
                    j, b = s - 2, s % 2
                    dve.wait_ge(S("exp_done"), j + 1)
                    if j >= 2:
                        dve.wait_ge(S("prob_ready"), j - 1)
                    dve.reciprocal(p_inv[:, b, 0:NT], p_sum[:, b, 0:NT]).then_inc(S("p_inv_ready"), 1)
                    dve.wait_ge(S("p_inv_ready"), j + 1)
                    dve.tensor_scalar(prob1[:, j % 3, :], prob1[:, j % 3, :], p_inv[:, b, 1:2], None,
                                      ALU.mult).then_inc(S("prob1_ready"), 1)
                if s < HEADS:
                    if s >= 2:
                        dve.wait_ge(S("scored"), s - 1)
                    dve.wait_ge(S("kq_psum"), 2 * s + 2)
                    rope(dve, B[5], [q_head[NOPE:QH, s % 2, :]], link)
                    dve.sem_inc(S("q_ready"), 1)
                if s >= 5 and s % 2:
                    k = (s - 5) // 2
                    dve.wait_ge(S("o_hi_ready"), k + 1)
                    dve.tensor_tensor(a_lo[:, k, :], B[7][:, 0:T], a_hi[:, k, :].bitcast(F32),
                                      ALU.subtract).then_inc(S("o_lo_ready"), 1)
                if 1 <= s <= HEADS:
                    j, b = s - 1, (s - 1) % 2
                    dve.wait_ge(S("scored"), j + 1)
                    for t, (_, rows) in enumerate(TOKEN_TILES):
                        last = dve.tensor_reduce(n_max[0:rows, b, t:t + 1], scores(b, t), AX.X, ALU.max)
                    link(last)
                    if j >= 2:
                        dve.wait_ge(S("exp_done"), j - 1)
                    dve.tensor_scalar(bias_e[:, b, 0:NT], n_max[:, b, 0:NT], -SCALE, None,
                                      ALU.mult).then_inc(S("bias_ready"), 1)
                if s % 4 in (1, 2):
                    lo_of(dve, U_H + s // 4 + 1, (s % 4 - 1,))
            residual_vector(dve, "ao_added", U_AO, 1)
            norm_inv(dve, "n3")
            for k in range(KD):
                dve.scalar_tensor_tensor(normed[:, k, :], h[:, k, :], prm("norm_ffn", KD + k), rstd[:, :],
                                         ALU.mult, ALU.mult).then_inc(S("n3_scaled"), 1)
            for i in range(2 * NT + 1):
                if i < 2 * NT:
                    t, rows = i // 2, TOKEN_TILES[i // 2][1]
                    dve.wait_ge(S("hf_0_ready"), i + 1)
                    if i >= 2:
                        dve.wait_ge(S("hf_2_ready"), i - 1)
                    dve.tensor_tensor(rest[0:rows, i % 2, :], B[i][0:rows, :], hf[0:rows, 0, t, HALVES[i % 2]],
                                      ALU.subtract).then_inc(S("hf_rest_ready"), 1)
                if i:
                    t, rows = (i - 1) // 2, TOKEN_TILES[(i - 1) // 2][1]
                    cols = HALVES[(i - 1) % 2]
                    dve.wait_ge(S("hf_1_ready"), i)
                    dve.tensor_tensor(hf[0:rows, 2, t, cols], rest[0:rows, (i - 1) % 2, :], hf[0:rows, 1, t, cols],
                                      ALU.subtract).then_inc(S("hf_2_ready"), 1)
            link(dve.memset(logit[:, :, :], 0.0))
            dve.wait_ge(S("logits_psum"), 1)
            dve.tensor_copy(logit[:, 0:2, :], B[6][:, 0:16].rearrange("p (t e) -> p t e", t=2))
            link(dve.tensor_copy(logit[0:16, 2, :], B[6][0:16, 16:24]))
            four = [P, NT, N_EXPERTS, N_EXPERTS]
            other = logit[:, :, :].unsqueeze(2).to_broadcast(four)
            self_ = logit[:, :, :].unsqueeze(3).to_broadcast(four)
            view = [c[:, :, :].rearrange("p t (e j) -> p t e j", e=N_EXPERTS) for c in (cmp_a, cmp_b)]
            dve.tensor_tensor(view[0], other, self_, ALU.is_gt)
            link(dve.tensor_tensor(view[1], other, self_, ALU.is_equal))
            tie = const[:, C_TIE:C_TIE + 64].unsqueeze(1).to_broadcast([P, NT, 64])
            link(dve.tensor_tensor(cmp_b[:, :, :], cmp_b[:, :, :], tie, ALU.mult))
            link(dve.tensor_tensor(cmp_a[:, :, :], cmp_a[:, :, :], cmp_b[:, :, :], ALU.add))
            link(dve.tensor_reduce(chosen[:, :, :], view[0], AX.X, ALU.add))
            dve.tensor_scalar(chosen[:, :, :], chosen[:, :, :], float(TOP_K), None, ALU.is_lt)\
                .then_inc(S("chosen_ready"), 1)
            link(dve.tensor_reduce(r_small[:, 0, :], logit[:, :, :], AX.X, ALU.max))
            three_e = [P, NT, N_EXPERTS]
            dve.tensor_tensor(r_exp[:, :, :], logit[:, :, :], r_small[:, 0, :].unsqueeze(2).to_broadcast(three_e),
                              ALU.subtract).then_inc(S("r_shifted"), 1)
            dve.wait_ge(S("r_exp_ready"), 1)
            dve.wait_ge(S("chosen_ready"), 1)
            link(dve.tensor_tensor(gate[:, :, :], r_exp[:, :, :], chosen[:, :, :], ALU.mult))
            link(dve.tensor_reduce(r_small[:, 1, :], gate[:, :, :], AX.X, ALU.add))
            link(dve.reciprocal(r_small[:, 2, :], r_small[:, 1, :]))
            link(dve.tensor_tensor(gate[:, :, :], gate[:, :, :],
                                   r_small[:, 2, :].unsqueeze(2).to_broadcast(three_e), ALU.mult))
            link(dve.memset(place[:, :, :], -1.0))
            link(dve.memset(place_1[:, :, :], 0.0))
            dve.wait_ge(S("ranks_psum"), 1)
            for t, (_, rows) in enumerate(TOKEN_TILES):
                last = dve.scalar_tensor_tensor(place_1[0:rows, t, :], B[5][0:rows, 8 * t:8 * t + 8], 1.0,
                                                chosen[0:rows, t, :], ALU.add, ALU.mult)
            link(last)
            for n in range(PASSES):
                last = dve.tensor_scalar(place[:, :, 8 * n:8 * n + 8], place_1[:, :, :], -1.0 - P * n, None, ALU.add)
            link(last)
            link(dve.tensor_reduce(r_small[0:1, 3, 0:1], B[5][0:1, 32:40], AX.X, ALU.max))
            pick_run(dve, 0)
            dve.tensor_copy(count_i[0:1, 0:1], r_small[0:1, 3, 0:1]).then_inc(S("count_ready"), 1)
            for n in range(3):
                src = gate if n == 0 else gate_rest
                link(dve.tensor_copy(gate_part[:, n, :, :], src[:, :, :]))
                if n < 2:
                    link(dve.tensor_tensor(gate_rest[:, :, :], src[:, :, :], gate_part[:, n, :, :], ALU.subtract))
            dve.sem_inc(S("gates_split"), 1)
            for u in range(SPLIT - 1):
                moe_lo(dve, 0, u)
            xe_lo_copy(dve, 0)
            moe_lo(dve, 0, SPLIT - 1)
            with dve.Fori(0, N_EXPERTS - 1) as m:
                run_vector(dve, m, m, False, True)
            run_vector(dve, N_EXPERTS - 1, N_EXPERTS - 1, False, False)
            overflow(dve, lambda m, e: run_vector(dve, m, e, True, False))
            link(dve.memset(ss[:, 0, :], 1.0))
            dve.drain().then_inc(S("acc_done"), 1)
            dve.wait_ge(S("last_std"), 1)
            link(dve.reciprocal(ss[:, 2, :], ss[:, 1, :]))
            dve.wait_ge(S("g_final_landed"), 16)
            for t, (_, rows) in enumerate(TOKEN_TILES):
                dve.scalar_tensor_tensor(y_out[0:rows, t, :], acc[0:rows, t, :], ss[0:rows, 2, t:t + 1],
                                         g_final[0:rows, :], ALU.mult, ALU.mult).then_inc(S("y_out_ready"), 1)

        @block.tensor
        def _(pe):
            pe.sem_inc(S("m_used"), SPLIT)
            pe.wait_ge(S("const_landed"), 16)
            pe.wait_ge(S("x_landed"), 64)
            for k in range(KD):
                for t, (t0, rows) in enumerate(TOKEN_TILES):
                    last = pe.transpose(B[k][:, t0:t0 + rows], x_rows[0:rows, t, k * P:(k + 1) * P],
                                        ident[0:rows, 0:rows])
                last.then_inc(S("x_transposed"), 1)
            pe.wait_ge(S("pool_set"), 1)
            for k in range(KD):
                norm_sum(pe, "n0", k, KD, B[0])
            pe.wait_ge(S("params_landed"), 160)
            pe.wait_ge(S("h0_ready"), 2)
            pe.transpose(B[1][:, 384:384 + N_PARAMS], p_rows[0:N_PARAMS, :],
                         ident[0:N_PARAMS, 0:N_PARAMS]).then_inc(S("params_transposed"), 1)

            def two_blocks(u, slot, banks2, block_ready=lambda k: None):
                pe.wait_ge(S("w_lo_ready"), u + 1)
                two_products(pe, slot, banks2, a_hi, a_lo, block_ready).then_inc(S("w_used"), 1)

            for u in range(4):
                if u >= 2:
                    pe.wait_ge(S("x_evacuated"), u - 1)
                two_blocks(U_X + u, (U_X + u) % 2, B[2 * (u % 2):2 * (u % 2) + 2],
                           lambda k: pe.wait_ge(S("n0_lo"), k + 1) if u == 0 else None)
            pe.wait_ge(S("x_evacuated"), 3)
            two_blocks(U_Y, U_Y % 2, B[0:2])
            pe.wait_ge(S("w_lo_ready"), U_G + 1)
            wh, wl = blocks_of(U_G % 2, 2048, 16)
            for k in range(N_BLOCKS):
                pe.wait_ge(S("xc_lo_ready"), k + 1)
                for g in range(2):
                    if k >= 2:
                        pe.wait_ge(S("gates_done"), 2 * (k - 2) + g + 1)
                    n = g * N_BLOCKS + k
                    last = three(pe, B[4 + (2 * k + g) % 4][:, 0:T], wh[:, n, :], wl[:, n, :], b_hi[:, k, :],
                                 b_lo[:, k, :], True, True)
                    last.then_inc(S("gate_psum"), 1)
            pe.wait_ge(S("gate_psum"), 2 * N_BLOCKS)
            pe.sem_inc(S("w_used"), 1)
            pe.wait_ge(S("x_evacuated"), 4)
            for q in range(3):
                if q == 1:
                    pe.wait_ge(S("gates_done"), 2 * N_BLOCKS)
                two_blocks(U_Y1 + q, (U_Y1 + q) % 2, B[2 * q + 2:2 * q + 4])
            residual_tensor(pe, "n1", "o_added", U_O, 4, 1, lambda q: dict(n=2048, k=8, xh=a_hi, xl=a_lo),
                            lambda k: pe.wait_ge(S("mixed_lo"), k + 1))
            with pe.Fori(0, KF // 2) as i:
                pe.wait_ge(S("silu_ready"), i + 1)
                two_blocks(U_F + 2 * i, U_F % 2, B[0:2], lambda k: pe.wait_ge(S("n1_lo"), k + 1))
                pe.wait_ge(S("g_ready"), 2 * i + 2)
                two_blocks(U_F + 1 + 2 * i, (U_F + 1) % 2, B[2:4])
            pe.wait_ge(S("silu_ready"), KF // 2 + 1)
            pe.wait_ge(S("g_lo_ready"), KF // 2)

            def down_unit(q):
                if q == 1:
                    pe.wait_ge(S("g_lo_ready"), KF // 2 + 1)
                return dict(n=11 * 256, k=11, xh=g_hi, xl=g_lo, x0=11 * (q % 2), first=q % 2 == 0, last=q % 2 == 1)

            residual_tensor(pe, "n2", "w2_added", U_W2, 8, 2, down_unit)
            pe.wait_ge(S("w_lo_ready"), U_KV + 1)
            wh, wl = blocks_of(U_KV % 2, 8 * 320, KD)
            for k in range(KD):
                pe.wait_ge(S("n2_lo"), k + 1)
                for n, col in enumerate((0, P, 192)):
                    last = three(pe, B[n][:, 0:T], wh[:, k, col:col + P], wl[:, k, col:col + P], a_hi[:, k, :],
                                 a_lo[:, k, :], k == 0, k == KD - 1)
            last.then_inc(S("w_used"), 1)
            pe.wait_ge(S("n2b_lo"), KD)
            pe.wait_ge(S("w_lo_ready"), U_Q + 1)
            for n in range(KQ):
                last = product(pe, U_Q % 2, 3072, 8, P * n, B[3 + n], b_hi, b_lo)
                if n == 1:
                    for k in range(KC):
                        norm_sum(pe, "nk", k, KC, B[7])
            last.then_inc(S("w_used"), 1)
            for k in range(KQ):
                norm_sum(pe, "nq", k, KQ, B[6])
            pe.wait_ge(S("nk_lo"), KC)
            for s in range(HEADS + 4):
                if s < HEADS:
                    g, hh = s // 4, s % 4
                    slot = (U_H + g) % 2
                    kh, kl = (w[:, slot, 0:1024].rearrange("p (k n) -> p k n", k=KC) for w in (w_hi, w_lo))
                    qh, ql = (w[:, slot, 1024:1024 + 12 * P].rearrange("p (k n) -> p k n", k=KQ)
                              for w in (w_hi, w_lo))
                    if s:
                        pe.wait_ge(S("kq_ready"), s)
                        pe.wait_ge(S("q_ready"), s)
                    if hh == 0:
                        pe.wait_ge(S("w_lo_ready"), U_H + g + 1)
                        vh, vl = (w.rearrange("p k (h n) -> p k h n", h=4)[:, :, :, NOPE:NOPE + VH] for w in (kh, kl))
                        for t, (t0, rows) in enumerate(TOKEN_TILES):
                            o = (B[4][0:rows, 0:256], B[4][0:rows, 256:512], B[5][0:rows, 0:256])[t]
                            o = o.rearrange("p (h n) -> p h n", h=4)
                            for k in range(KC):
                                last = moving(pe, o, c_hi[:, k, t0:t0 + rows], c_lo[:, k, t0:t0 + rows],
                                              vh[:, k], vl[:, k], k == 0, k == KC - 1)
                        last.then_inc(S("v_psum"), 1)
                        pe.wait_ge(S("v_ready"), g + 1)
                    for k in range(KC):
                        c0 = hh * (NOPE + VH)
                        last = three(pe, B[4][0:NOPE, 0:T], kh[:, k, c0:c0 + NOPE], kl[:, k, c0:c0 + NOPE],
                                     c_hi[:, k, :], c_lo[:, k, :], k == 0, k == KC - 1)
                    last.then_inc(S("kq_psum"), 1)
                    if s == 0:
                        pe.wait_ge(S("nq_lo"), KQ)
                    for k in range(KQ):
                        c0 = hh * P
                        last = three(pe, B[5][:, 0:T], qh[:, k, c0:c0 + P], ql[:, k, c0:c0 + P], cq_hi[:, k, :],
                                     cq_lo[:, k, :], k == 0, k == KQ - 1)
                    last.then_inc(S("kq_psum"), 1)
                    if hh == 3:
                        pe.wait_ge(S("kq_psum"), 2 * s + 2)
                        pe.sem_inc(S("w_used"), 1)
                if s >= 4:
                    j, b = s - 4, s % 2
                    pe.wait_ge(S("probT_ready"), j + 1)
                    if j >= 2 and j % 2 == 0:
                        pe.wait_ge(S("o_lo_ready"), j // 2)
                    g, c0, o0 = (j // 4) % 2, (j % 4) * VH, (j % 2) * VH
                    o = B[7][o0:o0 + VH, 0:T]
                    pe.matmul(o, v_sb[:, g, 0, c0:c0 + VH], probT[:, b, 0:T], start=True, stop=False)
                    pe.matmul(o[:, 64:T], v_sb[:, g, 1, c0:c0 + VH], probT[:, b, T:T + 208], start=False, stop=False)
                    pe.matmul(o[:, 192:T], v_sb[0:16, g, 2, c0:c0 + VH], probT2[0:16, b, :], start=False,
                              stop=True).then_inc(S("weighted"), 1)
                if 1 <= s <= HEADS:
                    j, b = s - 1, (s - 1) % 2
                    if j == 0:
                        pe.wait_ge(S("mask_rows"), 1)
                    pe.wait_ge(S("kq_ready"), j + 1)
                    pe.wait_ge(S("q_ready"), j + 1)
                    if j >= 2:
                        pe.wait_ge(S("exp_done"), j - 1)
                    n = QH + N_CHUNKS
                    for t, (t0, rows) in enumerate(TOKEN_TILES):
                        o = scores(b, t)
                        last = pe.matmul(o, q_head[0:n, b, t0:t0 + rows], k_head[0:n, b, 0:o.shape[1]],
                                         start=True, stop=True)
                    last.then_inc(S("scored"), 1)
                if 3 <= s < HEADS + 3:
                    j, r = s - 3, s % 3
                    pe.wait_ge(S("prob_ready"), j + 1)
                    pe.wait_ge(S("prob1_ready"), j + 1)
                    TP, OP = B[6], B[7]
                    pe.transpose(TP[:, 0:P], prob0[:, r, 0:P], ident)
                    pe.transpose(TP[:, P:2 * P], prob1[:, r, 0:P], ident)
                    pe.transpose(TP[:, 2 * P:T], prob2[0:16, r, 0:P], ident[0:16, 0:16])
                    pe.transpose(TP[:, T:T + 64], prob0[64:P, r, P:2 * P], ident[64:P, 64:P])
                    pe.transpose(TP[:, T + 64:T + 192], prob1[:, r, P:2 * P], ident)
                    pe.transpose(TP[:, T + 192:T + 208], prob2[0:16, r, P:2 * P], ident[0:16, 0:16])
                    if j >= 2 and j % 2 == 0:
                        pe.wait_ge(S("o_lo_ready"), j // 2)
                    pe.transpose(OP[0:16, T:T + 64], prob1[64:P, r, 2 * P:T], ident[64:P, 64:P])
                    pe.transpose(OP[0:16, T + 64:T + 80], prob2[0:16, r, 2 * P:T],
                                 ident[0:16, 0:16]).then_inc(S("p_transposed"), 1)
            residual_tensor(pe, "n3", "ao_added", U_AO, 4, 1, lambda q: dict(n=2048, k=8, xh=a_hi, xl=a_lo),
                            lambda k: pe.wait_ge(S("o_lo_ready"), k + 1))
            for name, src in (("h_rows", h), ("hf_rows", normed)):
                for i in range(2 * NT):
                    t0, rows = TOKEN_TILES[i // 2]
                    if src is normed:
                        pe.wait_ge(S("acc_set"), i + 1)
                        pe.wait_ge(S("n3_scaled"), 4 + 4 * (i % 2))
                    for kk in range(4):
                        k = 4 * (i % 2) + kk
                        last = pe.transpose(B[i][0:rows, kk * P:(kk + 1) * P], src[:, k, t0:t0 + rows], ident)
                    last.then_inc(S(name), 1)
            pe.wait_ge(S("router_landed"), 16)
            pe.wait_ge(S("n3_scaled"), KD)
            for t, (t0, rows) in enumerate(TOKEN_TILES):
                for k in range(KD):
                    last = pe.matmul(B[6][0:rows, 8 * t:8 * t + 8], normed[:, k, t0:t0 + rows], router[:, k, :],
                                     start=k == 0, stop=k == KD - 1)
            last.then_inc(S("logits_psum"), 1)
            pe.wait_ge(S("chosen_ready"), 1)
            pe.wait_ge(S("hf_2_ready"), 2 * NT)
            pe.wait_ge(S("ident_b_ready"), 1)
            tri = const[:, C_TRI:C_TRI + P]
            for t, (_, rows) in enumerate(TOKEN_TILES):
                for tt in range(t + 1):
                    r = TOKEN_TILES[tt][1]
                    pe.matmul(B[5][0:rows, 8 * t:8 * t + 8], (tri if tt == t else ones)[0:r, 0:rows],
                              chosen[0:r, tt, :], start=tt == 0, stop=tt == t)
            for tt, (_, r) in enumerate(TOKEN_TILES):
                last = pe.matmul(B[5][:, 32:40], ones[0:r, :], chosen[0:r, tt, :], start=tt == 0, stop=tt == NT - 1)
            last.then_inc(S("ranks_psum"), 1)
            pe.wait_ge(S("pick_ready"), 1)
            gather(pe, 0)
            with pe.Fori(0, N_EXPERTS - 1) as m:
                run_tensor(pe, m, False, True)
            run_tensor(pe, N_EXPERTS - 1, False, False)
            overflow(pe, lambda m, e: run_tensor(pe, m, True, False))


_INS = ["x", "meta_tokens", "norm_mix", "norm_ffn", "norm_final", "rnn_w_in", "rnn_conv_w", "rnn_conv_b",
        "rnn_w_a", "rnn_b_a", "rnn_w_i", "rnn_b_i", "rnn_lambda", "rnn_w_out", "kv_norm_src", "kv_w_down",
        "kv_latent_norm", "kv_w_up", "q_w_down", "q_latent_norm", "q_w_up", "attn_w_out", "ffn_w1", "ffn_w3",
        "ffn_w2", "moe_router", "moe_w1", "moe_w3", "moe_w2"]


def kernel(**inputs):
    import concourse.bacc as bacc
    from concourse.bass_utils import run_bass_kernel_spmd

    nc = bacc.Bacc("TRN2", target_bir_lowering=False, num_devices=1)
    arrays, args = {}, []
    for name in _INS:
        a = np.ascontiguousarray(inputs[name])
        arrays[f"in_{name}"] = a
        args.append(nc.dram_tensor(f"in_{name}", a.shape, mybir.dt.from_np(a.dtype), kind="ExternalInput").ap())
    arrays["consts"] = shape_constants()
    args.append(nc.dram_tensor("consts", (P, N_CONST), F32, kind="ExternalInput").ap())
    args.append(nc.dram_tensor("out", (1, SEQ, D), F32, kind="ExternalOutput").ap())
    trunk(nc, *args)
    r = run_bass_kernel_spmd(nc, [arrays], core_ids=[0])
    return r.results[0]["out"]
```
